# Optimizing a Trainium2 kernel written in Bass

```python
import math
import jax, jax.numpy as jnp
from jax import lax
import numpy as np

D_MODEL = 1024
BATCH = 1
SEQ = 1024
DEPTH = 1

A_GROUPS = 4
A_GROUP_CH = 128
A_CHUNK = 128
A_WIDTH = A_GROUPS * A_GROUP_CH
B_HEADS = 4
B_HEAD_DIM = 128
B_CONV = 4
B_CHUNK = 64
B_WIDTH = B_HEADS * B_HEAD_DIM
C_PATTERNS = ((128, 1), (512, 4), (2048, 16))
C_GROUPS = 3
C_HEADS = 4
C_HEAD_DIM = 128
C_BLOCK = 128
C_WIDTH = C_HEADS * C_HEAD_DIM
C_QK_W = C_GROUPS * C_WIDTH
REL_BUCKETS = 32
REL_MAX_DIST = 2048
N_BRANCH = 3
BRANCH_W = 512
N_IN = 2 * A_WIDTH + 4 * B_WIDTH + 2 * B_HEADS + 2 * C_QK_W + C_WIDTH + N_BRANCH * D_MODEL
MOE_GROUPS = 4
MOE_EXPERTS_PER_GROUP = 8
MOE_EXPERTS = MOE_GROUPS * MOE_EXPERTS_PER_GROUP
MOE_TOPK = 2
MOE_FF = 512
MOE_BLOCK = 128
EPS = 1e-6

kernel_name = 'hybrid_gated_parallel_mixers_hier_moe'

def rmsnorm(x, g):
    xf = x.astype(jnp.float32)
    y = xf * lax.rsqrt(jnp.mean(xf * xf, axis=-1, keepdims=True) + EPS)
    return y.astype(x.dtype) * g

def layernorm(x, g, b):
    xf = x.astype(jnp.float32)
    mu = jnp.mean(xf, axis=-1, keepdims=True)
    xc = xf - mu
    y = xc * lax.rsqrt(jnp.mean(xc * xc, axis=-1, keepdims=True) + EPS)
    return y.astype(x.dtype) * g + b

def l2norm(x):
    return x * lax.rsqrt(jnp.sum(x * x, axis=-1, keepdims=True) + EPS)

def spatial_gating_mixer(u, v, w_s, b_s, ln_g, ln_b):
    B, T, _ = u.shape
    u = jax.nn.gelu(u)
    v = layernorm(jax.nn.gelu(v), ln_g, ln_b)
    v = v.reshape(B, T // A_CHUNK, A_CHUNK, A_GROUPS, A_GROUP_CH)
    w = jnp.where(np.tril(np.ones((A_CHUNK, A_CHUNK), dtype=bool)), w_s, 0.0)
    sv = jnp.einsum('gts,bnsgc->bntgc', w, v) + jnp.transpose(b_s)[:, :, None]
    return u * sv.reshape(B, T, A_WIDTH)

def causal_depthwise_conv(x, w):
    K, C = w.shape
    return lax.conv_general_dilated(x, w[:, None, :].astype(x.dtype), window_strides=(1,),
                                    padding=[(K - 1, 0)], dimension_numbers=('NWC', 'WIO', 'NWC'),
                                    feature_group_count=C)

def chunked_gated_delta_rule(q, k, v, g, beta):
    B, T, H, dk = q.shape
    dv = v.shape[-1]
    C = B_CHUNK
    NC = T // C
    f32 = jnp.float32
    q = l2norm(q.astype(f32)) * (dk ** -0.5)
    k = l2norm(k.astype(f32))
    v = v.astype(f32)

    def chunk(a):
        return a.reshape(B, NC, C, H, a.shape[-1]).transpose(0, 3, 1, 2, 4)

    q, k, v = chunk(q), chunk(k), chunk(v)
    g = g.astype(f32).reshape(B, NC, C, H).transpose(0, 3, 1, 2)
    beta = beta.astype(f32).reshape(B, NC, C, H).transpose(0, 3, 1, 2)
    gc = jnp.cumsum(g, axis=-1)
    incl = np.tril(np.ones((C, C), dtype=bool))
    strict = np.tril(np.ones((C, C), dtype=bool), -1)
    decay = jnp.exp(jnp.where(incl, gc[..., :, None] - gc[..., None, :], -jnp.inf))
    kb = k * beta[..., None]
    vb = v * beta[..., None]
    lower = jnp.where(strict, jnp.einsum('bhnid,bhnjd->bhnij', kb, k) * decay, 0.0)
    a_mat = lower + jnp.eye(C, dtype=f32)
    rhs = jnp.concatenate([vb, kb * jnp.exp(gc)[..., None]], axis=-1)
    sol = lax.linalg.triangular_solve(a_mat, rhs, left_side=True, lower=True, unit_diagonal=True)
    u, w = sol[..., :dv], sol[..., dv:]
    attn = jnp.where(incl, jnp.einsum('bhnid,bhnjd->bhnij', q, k) * decay, 0.0)
    q_dec = q * jnp.exp(gc)[..., None]
    g_last = gc[..., -1]
    k_dec = k * jnp.exp(g_last[..., None] - gc)[..., None]

    def step(S, xs):
        q_i, attn_i, u_i, w_i, k_i, gl_i = xs
        v_new = u_i - jnp.einsum('bhcd,bhde->bhce', w_i, S)
        o = jnp.einsum('bhcd,bhde->bhce', q_i, S) + jnp.einsum('bhij,bhje->bhie', attn_i, v_new)
        S = S * jnp.exp(gl_i)[..., None, None] + jnp.einsum('bhcd,bhce->bhde', k_i, v_new)
        return S, o

    xs = (jnp.moveaxis(q_dec, 2, 0), jnp.moveaxis(attn, 2, 0), jnp.moveaxis(u, 2, 0),
          jnp.moveaxis(w, 2, 0), jnp.moveaxis(k_dec, 2, 0), jnp.moveaxis(g_last, -1, 0))
    S0 = jnp.zeros((B, H, dk, dv), f32)
    _, o = lax.scan(step, S0, xs)
    return o.transpose(1, 0, 3, 2, 4).reshape(B, T, H, dv)

def gated_deltanet_mixer(q, k, v, z, beta_logit, alpha_logit, conv_w, a_log, dt_bias, norm_g):
    B, T, _ = q.shape
    qkv = jax.nn.silu(causal_depthwise_conv(jnp.concatenate([q, k, v], axis=-1), conv_w))
    q, k, v = jnp.split(qkv, 3, axis=-1)
    shp = (B, T, B_HEADS, B_HEAD_DIM)
    beta = jax.nn.sigmoid(beta_logit.astype(jnp.float32))
    g = -jnp.exp(a_log.astype(jnp.float32)) * jax.nn.softplus(alpha_logit.astype(jnp.float32) + dt_bias.astype(jnp.float32))
    o = chunked_gated_delta_rule(q.reshape(shp), k.reshape(shp), v.reshape(shp), g, beta).astype(q.dtype)
    o = rmsnorm(o, norm_g) * jax.nn.silu(z.reshape(shp))
    return o.reshape(B, T, B_WIDTH)

def _t5_bucket(dist):
    max_exact = REL_BUCKETS // 2
    n = np.maximum(dist, 0)
    large = max_exact + (np.log(np.maximum(n, 1) / max_exact) / math.log(REL_MAX_DIST / max_exact)
                         * (REL_BUCKETS - max_exact)).astype(np.int32)
    large = np.minimum(large, REL_BUCKETS - 1)
    return np.where(n < max_exact, n, large).astype(np.int32)

def _band_pattern(window, dil):
    i = np.arange(C_BLOCK)[:, None]
    kk = np.arange(2 * C_BLOCK)[None, :]
    j = C_BLOCK + i - kk
    band = (j >= 0) & (j <= window // dil)
    bucket = _t5_bucket(np.clip(j, 0, None) * dil)
    return band, bucket

def dilated_window_attention(q, k, v, bias, band, dil):
    B, T, H, dh = q.shape
    L = T // dil
    nblk = -(-L // C_BLOCK)
    Lp = nblk * C_BLOCK

    def to_blocks(a):
        a = jnp.swapaxes(a.reshape(B, L, dil, H, dh), 1, 2)
        a = jnp.pad(a, ((0, 0), (0, 0), (0, Lp - L), (0, 0), (0, 0)))
        return a.reshape(B, dil, nblk, C_BLOCK, H, dh)

    def with_prev(a):
        prev = jnp.pad(a, ((0, 0), (0, 0), (1, 0), (0, 0), (0, 0), (0, 0)))[:, :, :-1]
        return jnp.concatenate([prev, a], axis=3)

    qb = to_blocks(q)
    kb = with_prev(to_blocks(k))
    vb = with_prev(to_blocks(v))
    logits = jnp.einsum('brnqhd,brnkhd->brnhqk', qb, kb, preferred_element_type=jnp.float32) * (dh ** -0.5) + bias
    first = np.arange(2 * C_BLOCK) >= C_BLOCK
    valid = band[None] & ((np.arange(nblk) > 0)[:, None, None] | first[None, None, :])
    logits = jnp.where(valid[:, None], logits, -jnp.inf)
    mx = jnp.max(logits, axis=-1)
    p = jnp.exp(logits - mx[..., None])
    den = jnp.sum(p, axis=-1)
    num = jnp.einsum('brnhqk,brnkhd->brnqhd', p, vb.astype(jnp.float32))

    def from_blocks(a):
        a = a.reshape((B, dil, Lp) + a.shape[4:])[:, :, :L]
        return jnp.swapaxes(a, 1, 2).reshape((B, T) + a.shape[3:])

    return from_blocks(num), from_blocks(jnp.swapaxes(den, 3, 4)), from_blocks(jnp.swapaxes(mx, 3, 4))

def dilated_attention_mixer(q, k, v, rel_bias):
    B, T, _ = q.shape
    q = q.reshape(B, T, C_GROUPS, C_HEADS, C_HEAD_DIM)
    k = k.reshape(B, T, C_GROUPS, C_HEADS, C_HEAD_DIM)
    v = v.reshape(B, T, C_HEADS, C_HEAD_DIM)
    nums, dens, maxs = [], [], []
    for gi, (window, dil) in enumerate(C_PATTERNS):
        band, bucket = _band_pattern(window, dil)
        bias = jnp.transpose(rel_bias[bucket][..., gi * C_HEADS:(gi + 1) * C_HEADS], (2, 0, 1)).astype(jnp.float32)
        num, den, mx = dilated_window_attention(q[:, :, gi], k[:, :, gi], v, bias, band, dil)
        nums.append(num)
        dens.append(den)
        maxs.append(mx)
    maxs = jnp.stack(maxs)
    scale = jnp.exp(maxs - jnp.max(maxs, axis=0, keepdims=True))
    num = jnp.sum(scale[..., None] * jnp.stack(nums), axis=0)
    den = jnp.sum(scale * jnp.stack(dens), axis=0)
    out = num / den[..., None]
    return out.reshape(B, T, C_WIDTH).astype(v.dtype)

def hierarchical_moe(h, w_group, w_expert, w1, w3, w2):
    B, T, D = h.shape
    N = B * T
    xt = h.reshape(N, D)
    grp_prob = jax.nn.softmax(jnp.einsum('nd,dg->ng', xt, w_group).astype(jnp.float32), axis=-1)
    grp_p, grp_idx = lax.top_k(grp_prob, 1)
    exp_logits = jnp.einsum('nd,de->ne', xt, w_expert).astype(jnp.float32).reshape(N, MOE_GROUPS, MOE_EXPERTS_PER_GROUP)
    sel_logits = jnp.take_along_axis(exp_logits, grp_idx[:, :, None], axis=1)[:, 0]
    sel_prob = jax.nn.softmax(sel_logits, axis=-1)
    top_p, top_i = lax.top_k(sel_prob, MOE_TOPK)
    gate = grp_p * (top_p / jnp.sum(top_p, axis=-1, keepdims=True))
    expert = grp_idx * MOE_EXPERTS_PER_GROUP + top_i

    A = N * MOE_TOPK
    e = expert.reshape(A)
    tok = jnp.repeat(jnp.arange(N, dtype=jnp.int32), MOE_TOPK)
    gw = gate.reshape(A)
    order = jnp.argsort(e)
    e_s, tok_s, gw_s = e[order], tok[order], gw[order]
    counts = jnp.bincount(e, length=MOE_EXPERTS)
    padded = (counts + MOE_BLOCK - 1) // MOE_BLOCK * MOE_BLOCK
    pad_end = jnp.cumsum(padded)
    pad_start = pad_end - padded
    start = jnp.cumsum(counts) - counts
    dest = pad_start[e_s] + jnp.arange(A) - start[e_s]
    R = A + MOE_EXPERTS * MOE_BLOCK
    row_tok = jnp.zeros((R,), jnp.int32).at[dest].set(tok_s)
    row_gate = jnp.zeros((R,), jnp.float32).at[dest].set(gw_s)
    n_blocks = R // MOE_BLOCK
    blk_expert = jnp.minimum(jnp.searchsorted(pad_end, jnp.arange(n_blocks) * MOE_BLOCK, side='right'), MOE_EXPERTS - 1)
    xb = xt[row_tok].reshape(n_blocks, MOE_BLOCK, D)

    def expert_block(args):
        xblk, eid = args
        hid = jax.nn.silu(xblk @ w1[eid]) * (xblk @ w3[eid])
        return hid @ w2[eid]

    yb = lax.map(expert_block, (xb, blk_expert)).reshape(R, D)
    y = jnp.zeros((N, D), h.dtype).at[row_tok].add(yb * row_gate[:, None].astype(yb.dtype))
    return y.reshape(B, T, D)

def setup_inputs(seed: int = 0) -> dict:
    key = jax.random.key(seed)
    ks = jax.random.split(key, 24)
    f32 = jnp.float32

    def nrm(k, shape, scale):
        return jax.random.normal(k, shape, f32) * scale

    x = nrm(ks[0], (BATCH, SEQ, D_MODEL), 1.0)
    norm_mix_g = 1.0 + nrm(ks[1], (DEPTH, D_MODEL), 0.02)
    w_in = nrm(ks[2], (DEPTH, D_MODEL, N_IN), D_MODEL ** -0.5)
    a_ln_g = 1.0 + nrm(ks[3], (DEPTH, A_WIDTH), 0.02)
    a_ln_b = nrm(ks[4], (DEPTH, A_WIDTH), 0.02)
    a_w_s = nrm(ks[5], (DEPTH, A_GROUPS, A_CHUNK, A_CHUNK), A_CHUNK ** -0.5)
    a_b_s = 1.0 + nrm(ks[6], (DEPTH, A_GROUPS, A_CHUNK), 0.1)
    b_conv_w = nrm(ks[7], (DEPTH, B_CONV, 3 * B_WIDTH), B_CONV ** -0.5)
    b_a_log = jnp.log(jax.random.uniform(ks[8], (DEPTH, B_HEADS), f32, 1.0, 16.0))
    dt = jnp.exp(jax.random.uniform(ks[9], (DEPTH, B_HEADS), f32, math.log(1e-3), math.log(1e-1)))
    b_dt_bias = dt + jnp.log(-jnp.expm1(-dt))
    b_norm_g = 1.0 + nrm(ks[10], (DEPTH, B_HEAD_DIM), 0.02)
    rel_bias = nrm(ks[11], (REL_BUCKETS, C_GROUPS * C_HEADS), 0.5)
    w_branch = nrm(ks[12], (DEPTH, N_BRANCH, BRANCH_W, D_MODEL), BRANCH_W ** -0.5)
    w_out = nrm(ks[13], (DEPTH, D_MODEL, D_MODEL), D_MODEL ** -0.5)
    norm_ffn_g = 1.0 + nrm(ks[14], (DEPTH, D_MODEL), 0.02)
    w_group = nrm(ks[15], (DEPTH, D_MODEL, MOE_GROUPS), D_MODEL ** -0.5)
    w_expert = nrm(ks[16], (DEPTH, D_MODEL, MOE_EXPERTS), D_MODEL ** -0.5)
    w1 = nrm(ks[17], (DEPTH, MOE_EXPERTS, D_MODEL, MOE_FF), D_MODEL ** -0.5)
    w3 = nrm(ks[18], (DEPTH, MOE_EXPERTS, D_MODEL, MOE_FF), D_MODEL ** -0.5)
    w2 = nrm(ks[19], (DEPTH, MOE_EXPERTS, MOE_FF, D_MODEL), MOE_FF ** -0.5)
    final_norm_g = 1.0 + nrm(ks[20], (D_MODEL,), 0.02)
    return {'x': x, 'norm_mix_g': norm_mix_g, 'w_in': w_in, 'a_ln_g': a_ln_g, 'a_ln_b': a_ln_b,
            'a_w_s': a_w_s, 'a_b_s': a_b_s, 'b_conv_w': b_conv_w, 'b_a_log': b_a_log,
            'b_dt_bias': b_dt_bias, 'b_norm_g': b_norm_g, 'rel_bias': rel_bias, 'w_branch': w_branch,
            'w_out': w_out, 'norm_ffn_g': norm_ffn_g, 'w_group': w_group, 'w_expert': w_expert,
            'w1': w1, 'w3': w3, 'w2': w2, 'final_norm_g': final_norm_g}

def reference(x, norm_mix_g, w_in, a_ln_g, a_ln_b, a_w_s, a_b_s, b_conv_w, b_a_log, b_dt_bias,
              b_norm_g, rel_bias, w_branch, w_out, norm_ffn_g, w_group, w_expert, w1, w3, w2,
              final_norm_g):
    B, T, D = x.shape
    sizes = [A_WIDTH, A_WIDTH, B_WIDTH, B_WIDTH, B_WIDTH, B_WIDTH, B_HEADS, B_HEADS,
             C_QK_W, C_QK_W, C_WIDTH, N_BRANCH * D_MODEL]
    splits = [int(s) for s in np.cumsum(sizes)[:-1]]
    for l in range(DEPTH):
        h = rmsnorm(x, norm_mix_g[l])
        proj = jnp.einsum('btd,dn->btn', h, w_in[l])
        (a_u, a_v, b_q, b_k, b_v, b_z, b_beta, b_alpha, c_q, c_k, c_v, gates) = jnp.split(proj, splits, axis=-1)
        y_a = spatial_gating_mixer(a_u, a_v, a_w_s[l], a_b_s[l], a_ln_g[l], a_ln_b[l])
        y_b = gated_deltanet_mixer(b_q, b_k, b_v, b_z, b_beta, b_alpha, b_conv_w[l], b_a_log[l],
                                   b_dt_bias[l], b_norm_g[l])
        y_c = dilated_attention_mixer(c_q, c_k, c_v, rel_bias)
        gates = jax.nn.sigmoid(gates.reshape(B, T, N_BRANCH, D))
        merged = (gates[:, :, 0] * (y_a @ w_branch[l, 0])
                  + gates[:, :, 1] * (y_b @ w_branch[l, 1])
                  + gates[:, :, 2] * (y_c @ w_branch[l, 2]))
        x = x + merged @ w_out[l]
        h = rmsnorm(x, norm_ffn_g[l])
        x = x + hierarchical_moe(h, w_group[l], w_expert[l], w1[l], w3[l], w2[l])
    return rmsnorm(x, final_norm_g)


_drawn_inputs = setup_inputs


def setup_inputs(seed=0):
    import zlib

    import numpy as np

    out = dict(_drawn_inputs(seed))
    spreads = {}
    factors = {'a_ln_g': 15.534,
     'a_ln_b': 16.755,
     'b_norm_g': 11.308,
     'final_norm_g': 8.739,
     'rel_bias': 2.89,
     'norm_ffn_g': 3.63}
    for name, (base, spread) in spreads.items():
        noise = np.random.default_rng([zlib.crc32(name.encode()), seed]).standard_normal(out[name].shape)
        drawn = base * np.exp(spread * noise) if base else spread * noise
        out[name] = __import__('jax').numpy.asarray(drawn.astype(out[name].dtype))
    for name, factor in factors.items():
        out[name] = (out[name] * factor).astype(out[name].dtype)
    return out
```

```python
import math
from contextlib import ExitStack, nullcontext

import numpy as np

import concourse.bass as bass
from concourse import mybir

F32 = mybir.dt.float32
F32R = mybir.dt.float32r
I32 = mybir.dt.int32
ALU = mybir.AluOpType
ACT = mybir.ActivationFunctionType
AX = mybir.AxisListType.X

P = 128
T = 1024
D = 1024
NT = T // P
KD = D // P
EPS = 1e-6
HALF = 512

CW = 256
N_TOK = 4
N_CH = 22
N_ABC = N_TOK + N_CH
N_GATE = 12
ROW_AU, ROW_BQ, ROW_BK, ROW_BV, ROW_BZ, ROW_CQ, ROW_CK = 0, 512, 1024, 1536, 2048, 2560, 4096
PT_ROWS = N_CH * CW

NH = 4
HD = 128
NC = NH * HD
REL_BUCKETS, REL_MAX_DIST = 32, 2048
PATTERNS = ((128, 1), (512, 4), (2048, 16))
BAND_COLS = (256, 640, 1024)
BAND_AT = (0, 256, 896)
BAND_ALL = sum(BAND_COLS)
BIAS_LEN = sum(c + P - 1 for c in BAND_COLS)
NEG = -1e30
NO_ROW = 4 * T
CHUNK = 64
LEVELS = 6
GROUP_SHIFTED, SECOND_SHIFTED, ONE_HOTS, ROUTER_STEPS = 3, 21, 26, 64


SBUF_END = 229368


class Region:

    def __init__(self, nc, base):
        self.nc, self.at = nc, base

    def __call__(self, name, shape, dt=F32):
        size = 4 * int(np.prod(shape[1:]))
        t = self.nc.alloc_sbuf_tensor_at(name, list(shape), dt, offset=self.at)
        self.at += (size + 31) // 32 * 32
        return t


def t5_bucket(dist):
    n = np.maximum(dist, 0)
    exact = REL_BUCKETS // 2
    large = exact + (np.log(np.maximum(n, 1) / exact) / math.log(REL_MAX_DIST / exact) * (REL_BUCKETS - exact)).astype(np.int32)
    return np.where(n < exact, n, np.minimum(large, REL_BUCKETS - 1)).astype(np.int32)


def bucket_selector():
    sel = np.zeros((REL_BUCKETS + 1, BIAS_LEN), np.float32)
    at = 0
    for (window, dil), cols in zip(PATTERNS, BAND_COLS):
        n = cols + P - 1
        delta = (cols - P) + (P - 1) - np.arange(n)
        ok = (delta >= 0) & (delta % dil == 0) & (delta <= window)
        b = t5_bucket(delta)
        sel[b[ok], at + np.arange(n)[ok]] = 1.0
        sel[REL_BUCKETS, at + np.arange(n)[~ok]] = NEG
        at += n
    return sel


class Chain:

    def __init__(self, eng, sem):
        self.eng, self.sem, self.n, self.i, self.per, self.start = eng, sem, 0, None, 0, 0

    def enter(self, i, per, first=0):
        self.n -= per * first
        self.i, self.per, self.start, self.first = i, per, self.n, first

    def leave(self, rounds):
        assert self.n - self.start == self.per, (self.n - self.start, self.per)
        self.n, self.i = self.start + self.per * (self.first + rounds), None

    def link(self, ins):
        ins.then_inc(self.sem, 1)
        self.n += 1
        self.eng.wait_ge(self.sem, self.n if self.i is None else self.i * self.per + self.n)


def build(nc, x, w_in_t, w_ba, g_mix, a_ws_t, a_bs, a_gb, sel, relb, conv_w, b_hv, b_ng, b_masks, w_br, w_o, g_ffn, w_r, iotas, tok_ids, w1, w3, w2, g_fin, out):
    ctx = ExitStack()
    with ctx:
        def sem(name):
            return nc.alloc_semaphore(name=name)

        base = (nc.sbuf_base + 31) // 32 * 32
        const = Region(nc, base)
        ident = const("ident", [P, P])
        ones = const("ones", [P, P])
        gmix_col = const("gmix_col", [P, KD])
        ss = const("ss", [P, NT])
        rs = const("rs", [P, NT])
        ba = const("ba", [P, NT, 8])
        b_mark = const("b_mark", [P, 1])
        rs_t = const("rs_t", [P, NT])
        gffn_col = const("gffn_col", [P, KD])
        gates2 = const("gates2", [P, NT, 2])
        dest = const("dest", [P, NT, 2], I32)
        END_CONST = const.at

        low = Region(nc, END_CONST)
        hT_h = low("hT_h", [P, KD, T], F32R)
        hT_l = low("hT_l", [P, KD, T], F32R)
        TOKV_AT = low.at
        tokv = low("tokv", [P, NT, N_TOK * CW])
        r1 = Region(nc, low.at)
        xs = r1("xs", [P, NT, D])
        r1b = Region(nc, low.at)
        wraw = r1b("wraw", [P, 2, KD, CW])
        r1c = Region(nc, max(r1.at, r1b.at))
        w_h = r1c("w_h", [P, 2, KD, CW], F32R)
        w_l = r1c("w_l", [P, 2, KD, CW], F32R)
        stage = r1c("stage", [P, 2, 2, T])
        junk = r1c("junk", [P, D])
        wba_raw = r1c("wba_raw", [P, KD, 8])
        wba_h = r1c("wba_h", [P, KD, 8], F32R)
        wba_l = r1c("wba_l", [P, KD, 8], F32R)

        psum = ctx.enter_context(nc.psum_tensor("psum", [P, 8 * HALF], F32))
        ps = [psum[:, b * HALF:(b + 1) * HALF] for b in range(8)]

        pt = nc.dram_tensor("pt_scratch", [PT_ROWS, T], F32).ap()

        s_x = sem("x_loaded")
        s_cst = sem("constants_made")
        s_gcol = sem("gains_loaded")
        s_ss = sem("sums_of_squares")
        s_ms = sem("mean_squares")
        s_rt = sem("roots")
        s_rs = sem("inverse_rms")
        s_xn = sem("x_normalized")
        s_xt = sem("x_transposed")
        s_hh = sem("h_high")
        s_hl = sem("h_low")
        s_wraw = [sem(f"w_raw_loaded{i}") for i in range(2)]
        s_wh = sem("w_high")
        s_wl = sem("w_low")
        s_grp = sem("projection_groups")
        s_ev = sem("projection_evacuated")
        s_st = [sem(f"stage_stored{i}") for i in range(2)]
        s_ba = sem("beta_alpha_loaded")
        s_bah = sem("beta_alpha_weights_split")
        s_phase = sem("phase_done")

        ys = nc.dram_tensor("y_scratch", [3 * NC, T], F32).ap()
        frs = nc.dram_tensor("bias_scratch", [12, BIAS_LEN], F32).ap()

        ra = Region(nc, low.at)
        aw = ra("aw", [P, NH, P])
        a_one = ra("a_one", [1, P])
        a_bias = ra("a_bias", [1, NC])
        a_gbt = ra("a_gbt", [P, 2, NC])
        a_u = ra("a_u", [P, NH, T])
        a_y = ra("a_y", [P, NH, T])
        a_sum = ra("a_sum", [P, NT])
        a_sq = ra("a_sq", [P, NT])
        a_junk = ra("a_junk", [P, NC])
        c_sel = ra("c_sel", [REL_BUCKETS + 1, BIAS_LEN])
        c_relb = ra("c_relb", [REL_BUCKETS + 1, 12])
        c_fr = ra("c_fr", [12, BIAS_LEN])
        s_aload = sem("gating_inputs_loaded")
        s_au = sem("u_loaded")
        s_amask = sem("gating_weights_masked")
        s_ag = sem("v_gelu")
        s_an = sem("v_normalized")
        s_asv = sem("gated_sums")
        s_aug = sem("u_gelu")
        s_ay = sem("y_a_made")
        s_asq = sem("v_squares")
        s_art = sem("v_roots")
        s_amu = sem("v_means")
        s_avs = sem("v_variances")
        s_ydma = sem("y_stored")
        s_frmm = sem("bias_vector_product")
        s_fr = sem("bias_vector_out")
        s_frd = sem("bias_vector_stored")
        s_cd = sem("dve_chain")
        s_ca = sem("act_chain")
        s_cp = sem("pool_chain")
        rc = Region(nc, low.at)
        c_q = rc("c_q", [P, 2, 3, T])
        c_k = rc("c_k", [P, 2, 3, T])
        c_tab = rc("c_tab", [P, 2, BAND_ALL])
        c_lg = rc("c_lg", [P, 3, BAND_ALL])
        c_pt = rc("c_pt", [P, 2, T])
        c_st = rc("c_st", [P, 4, 4])
        c_rows = rc("c_rows", [P, 2, NT, HD])
        c_yt = rc("c_yt", [P, 2, T])
        s_yst = [sem(f"attention_stored{u}") for u in range(2)]

        NCONV = 3 * NH
        NQ = 2 * NH
        rb = Region(nc, TOKV_AT)
        b_c = rb("b_c", [P, NCONV, T])
        b_m = rb("b_m", [P, 4 + LEVELS, P])
        U_INCL, M_CHUNK, M_FIRST, M_SECOND = (b_m[:, n] for n in range(4))
        b_cw = rb("b_cw", [P, NCONV, 4])
        b_hvt = rb("b_hvt", [P, 2, NH])
        b_ngt = rb("b_ngt", [P, 1])
        eb = rb("eb", [P, NT, NH])
        ea = rb("ea", [P, NH])
        xg = rb("xg", [P, NT, NH])
        xm = rb("xm", [P, NT, NH])
        xn = rb("xn", [P, NT, NH])
        xu = rb("xu", [P, NT, NH])
        xl = rb("xl", [P, NT, NH])
        xc = rb("xc", [P, NT, NH])
        qs = rb("qs", [P, NT, NQ])
        qr = rb("qr", [P, NT, NQ])
        qt_ = rb("qt_", [P, NT, NQ])
        gall = rb("gall", [P, 4, NT, NH])
        eall = rb("eall", [P, 4, NT, NH])
        SM = rb("SM", [P, NT, 16])
        PSC = rb("PSC", [P, NT, 28])
        LOOP_AT = rb.at
        rbc = Region(nc, LOOP_AT)
        b_raw = rbc("b_raw", [P, 2, T + 4])
        b_sq = rbc("b_sq", [P, 2, T])
        rbl = Region(nc, LOOP_AT)
        cur = rbl("cur", [P, 2, 28])
        kqv = rbl("kqv", [P, 2, NCONV, P])
        bcs = rbl("bcs", [P, 16, P])
        dE = rbl("dE", [P, 2, NH, P])
        AT = rbl("AT", [P, 2, NH, P])
        LT = rbl("LT", [P, 2, NH, P])
        vb = rbl("vb", [P, 2, NH, P])
        kbg = rbl("kbg", [P, 2, NH, P])
        kdec = rbl("kdec", [P, 2, NH, P])
        qdec = rbl("qdec", [P, 2, NH, P])
        CT = rbl("CT", [P, 2, 2, NH, P])
        dD = rbl("dD", [P, 2, NH, P])
        dR = rbl("dR", [P, 2, NH, P])
        dP = rbl("dP", [P, 2, NH, P])
        wTn = rbl("wTn", [P, 2, NH, P])
        S = rbl("S", [P, NH, P])
        vn = rbl("vn", [P, 2, NH, P])
        rbz = Region(nc, LOOP_AT)
        b_z = rbz("b_z", [P, NH, T])
        o_a = rbz("o_a", [P, 2, HALF])
        o_y = rbz("o_y", [P, 2, HALF])
        o_t = rbz("o_t", [P, 2, HALF])
        s_bload = sem("delta_constants_loaded")
        s_braw = [sem(f"conv_input_loaded{u}") for u in range(2)]
        s_bpad = sem("conv_padding")
        s_bconv = sem("conv_done")
        s_bsilu = sem("conv_silu")
        s_bsq = sem("qk_squares")
        s_bss = sem("qk_square_sums")
        s_bn = sem("small_math_act")
        s_bm = sem("small_math_dve")
        s_bgc = sem("gate_sums")
        s_bset = sem("tile_scalars_ready")
        s_bini = sem("state_cleared")
        s_pk = sem("tile_copied")
        s_p1 = sem("tile_products")
        s_dm = sem("decay_exponents")
        s_de = sem("decay")
        s_lt = sem("lower_transposed")
        s_qd = sem("q_decayed")
        s_a1 = sem("kv_token_major")
        s_ct = sem("level_masked")
        s_pp = sem("level_product")
        s_ps = sem("level_product_out")
        s_xy = sem("level_corrections")
        s_du = sem("inverse_updated")
        s_w = sem("w_product")
        s_wn = sem("w_out")
        s_v = sem("v_new_product")
        s_vn = sem("v_new_out")
        s_o = sem("o_product")
        s_oev = sem("o_out")
        s_sm = sem("state_product")
        s_su = sem("state_updated")
        s_zl = sem("z_loaded")
        s_oq = sem("o_squares")
        s_om = sem("o_mean_squares")
        s_oa = sem("o_variance")
        s_ol = sem("o_root")
        s_zs = sem("z_silu")
        s_yb = sem("y_b_made")

        def bheads(ap2):
            return ap2.rearrange("p (a n) -> p a n", a=1).to_broadcast([P, NH, P])

        def banks4(b):
            return ps[b].rearrange("p (h n) -> p h n", h=NH)

        def widths(qt):
            n = [min(c // P, qt + 1) for c in BAND_COLS]
            return n, [0, n[0] * P, (n[0] + n[1]) * P], sum(n) * P
        s_cin = [sem(f"qk_loaded{u}") for u in range(2)]
        s_lg = sem("logits")
        s_lb = sem("logits_biased")
        s_mx = sem("row_max")
        s_ex = sem("exponentials")
        s_pa = sem("groups_added")
        s_tp = sem("probs_transposed")
        s_pt2 = sem("probs_out_of_psum")
        s_pv = sem("weighted_values")
        s_rd = sem("denominators_inverted")
        s_yc = sem("attention_rows_out")
        s_yt = sem("attention_transposed")
        s_yo = sem("attention_channel_major")

        wt = w_in_t

        NB = D // P
        rg = Region(nc, TOKV_AT)
        merged = rg("merged", [P, KD, T])
        MERGED_END = rg.at
        y_raw = rg("y_raw", [P, NH, T])
        y_h = rg("y_h", [P, NH, T], F32R)
        y_l = rg("y_l", [P, NH, T], F32R)
        g_raw = rg("g_raw", [P, 2, KD, P])
        g_h = rg("g_h", [P, 2, KD, P], F32R)
        g_l = rg("g_l", [P, 2, KD, P], F32R)
        br_raw = rg("br_raw", [P, 2, NH, P])
        br_h = rg("br_h", [P, 2, NH, P], F32R)
        br_l = rg("br_l", [P, 2, NH, P], F32R)
        sig = rg("sig", [P, 2, HALF])
        prod = rg("prod", [P, 2, HALF])
        s_yl = sem("y_loaded")
        s_yh = sem("y_high")
        s_yl2 = sem("y_low")
        s_gr = [sem(f"gate_weights_loaded{u}") for u in range(2)]
        s_gh = sem("gate_weights_high")
        s_gl = sem("gate_weights_low")
        s_pm = sem("gate_branch_products")
        s_sg = sem("gates_made")
        s_mg = sem("merged")
        rw = Region(nc, END_CONST)
        m_h = rw("m_h", [P, KD, T], F32R)
        m_l = rw("m_l", [P, KD, T], F32R)
        rw2 = Region(nc, END_CONST)
        xn2 = rw2("xn2", [P, NT, D])
        h2T = rw2("h2T", [P, KD, T])
        rw3 = Region(nc, MERGED_END)
        x2 = Region(nc, (SBUF_END - 4 * NT * D) // 32 * 32)("x2", [P, NT, D])
        wo_raw = rw3("wo_raw", [P, 2, KD, CW])
        wo_h = rw3("wo_h", [P, 2, KD, CW], F32R)
        wo_l = rw3("wo_l", [P, 2, KD, CW], F32R)
        junk2 = rw3("junk2", [P, D])
        wr = rw3("wr", [P, KD, 36])
        iot = rw3("iot", [P, 96])
        strict = rw3("strict", [P, P])
        tids = rw3("tids", [P, 2, NT], I32)
        NBLK = (2 * T + 32 * P) // P
        zer = rw3("zer", [P, NBLK], I32)
        rr = Region(nc, TOKV_AT)
        lg = rr("r_lg", [P, NT, 36])
        gm = rr("r_gm", [P, NT, 1])
        gd = rr("r_gd", [P, NT, 4])
        gp = rr("r_gp", [P, NT, 1])
        cand = rr("r_cand", [P, NT, 8])
        cm = rr("r_cm", [P, NT, 1])
        goh = rr("r_goh", [P, NT, 4])
        selt = rr("r_selt", [P, NT, 4, 8])
        sl = rr("r_sl", [P, NT, 8])
        m1 = rr("r_m1", [P, NT, 1])
        m2 = rr("r_m2", [P, NT, 1])
        oh = rr("r_oh", [P, 2, NT, 8])
        O = rr("r_O", [P, 2, NT, 32])
        Osum = rr("r_Osum", [P, NT, 32])
        padi = rr("r_padi", [P, 32], I32)
        padf = rr("r_padf", [P, 32])
        pend = rr("r_pend", [P, 2, 32])
        rank = rr("r_rank", [P, NT, 32])
        dtmp = rr("r_dtmp", [P, NT, 32])
        dsum = rr("r_dsum", [P, NT, 2])
        ihi = rr("r_ihi", [P, 2, NT, 2], I32)
        fhi = rr("r_fhi", [P, 2, NT, 2])
        place = rr("r_place", [P, NT, 2], I32)
        bcmp = rr("r_bcmp", [P, NBLK, 32])
        bexf = rr("r_bexf", [P, NBLK])
        bexf_n = rr("r_bexf_n", [P, 1])
        s_mh = sem("merged_high")
        s_ml = sem("merged_low")
        s_wor = [sem(f"w_out_loaded{u}") for u in range(2)]
        s_woh = sem("w_out_high")
        s_wol = sem("w_out_low")
        s_po = sem("output_products")
        s_x2l = sem("x_reloaded")
        s_x2 = sem("x2_made")
        s_xn2 = sem("x2_normalized")
        s_x2d = sem("h2_stored")
        s_t2 = sem("x2_transposed")
        s_h2 = sem("h2_channel_major")
        s_rc = sem("router_constants_loaded")
        s_rm = sem("router_product")
        s_rd1 = sem("router_dve")
        s_ra = sem("router_act")
        s_rk = sem("ranks")
        s_rtz = sem("zero_rows_made")
        s_rtc = sem("row_table_cleared")
        s_rts = sem("row_table_scattered")
        s_rtl = sem("row_table_loaded")
        FF = HD * NH
        bexp = Region(nc, END_CONST)("r_bexp", [P, NBLK + 1], I32)
        rm = Region(nc, END_CONST + 4 * (NBLK + 8))
        rasg = rm("rasg", [P, NBLK], I32)
        rtok_all = rm("rtok", [P, NBLK + 1], I32)
        rtok = rtok_all[:, 0:NBLK]
        aidx = rm("aidx", [P, 1], I32)
        e_raw = rm("e_raw", [P, 6, 4 * FF])
        e_h = rm("e_h", [P, 6, 4 * FF], F32R)
        e_l = rm("e_l", [P, 6, 4 * FF], F32R)
        xb = rm("xb", [P, D])
        xr = rm("xr", [P, D])
        zero = rm("zero", [P, 1])
        bidx = rm("bidx", [P, 1], I32)
        xT_h = rm("xT_h", [P, KD, P], F32R)
        xT_l = rm("xT_l", [P, KD, P], F32R)
        sg = rm("sg", [P, FF])
        hid = rm("hid", [P, FF])
        hT2_h = rm("hT2_h", [P, 4, P], F32R)
        hT2_l = rm("hT2_l", [P, 4, P], F32R)
        yb = rm("yb", [P, D])
        assert rm.at <= (SBUF_END - 4 * NT * D) // 32 * 32, rm.at
        h2s = nc.dram_tensor("h2_scratch", [T, D], F32).ap()
        rts = nc.dram_tensor("row_table", [NBLK * P, 1], I32).ap()
        ybs = nc.dram_tensor("expert_rows", [2 * T, D], F32).ap()
        cleared = [s_x, s_xn, s_xt, s_hh, s_hl, s_wh, s_wl, s_grp, s_ev, s_ba, s_bah, *s_wraw,
                   s_aload, s_au, s_amask, s_ag, s_an, s_asv, s_aug, s_ay, s_asq, s_art, s_amu, s_avs, s_frmm, s_fr, s_frd, s_cp,
                   *s_cin, s_lg, s_lb, s_mx, s_ex, s_pa, s_tp, s_pt2, s_pv, s_rd, s_yc, s_yt, s_yo, *s_yst]
        again = [h.num for h in cleared]
        for h in cleared:
            nc.release_semaphore(h)

        def sem(name):
            return nc.alloc_semaphore(name=name, num=again.pop(0))

        s_er = [sem(f"expert_weights_loaded{c}") for c in range(6)]
        s_eh13, s_eh2 = sem("up_weights_high"), sem("down_weights_high")
        s_el13, s_el2 = sem("up_weights_low"), sem("down_weights_low")
        s_e13 = sem("up_chunks_used")
        s_e2 = sem("down_chunks_used")
        s_rix = sem("row_indices")
        s_xb = sem("rows_gathered")
        s_xr = sem("rows_staged")
        s_tx = sem("rows_transposed")
        s_xh = sem("rows_high")
        s_xl = sem("rows_low")
        s_si = sem("silu")
        s_hd = sem("hidden")
        s_th = sem("hidden_transposed")
        s_hh2 = sem("hidden_high")
        s_hl2 = sem("hidden_low")
        s_ye = sem("expert_rows_out")
        s_ys = sem("expert_rows_stored")
        rf = Region(nc, END_CONST)
        yg = rf("yg", [P, NT, 2, D])
        x3 = x2
        gfin = rf("gfin", [P, D])
        fjunk = rf("fjunk", [P, D])
        s_fg = [sem(f"rows_returned{t}") for t in range(NT)]
        s_fx = sem("final_gain_loaded")
        s_f3 = sem("x3_made")
        s_fo = sem("output_made")
        s_out = sem("output_stored")

        def inverse_rms(dve, n):
            dve.wait_ge(s_ss, (n + 1) * NT)
            nc.vector.tensor_scalar(ss[:], ss[:], 1.0 / D, EPS, ALU.mult, ALU.add).then_inc(s_ms, 1)
            dve.wait_ge(s_rt, n + 1)
            for a, f in enumerate((lambda: nc.vector.reciprocal(rs[:], rs[:]),
                                   lambda: nc.vector.tensor_tensor(rs_t[:], ss[:], rs[:], ALU.mult),
                                   lambda: nc.vector.tensor_tensor(rs_t[:], rs_t[:], rs[:], ALU.mult),
                                   lambda: nc.vector.tensor_scalar(rs_t[:], rs_t[:], -0.5, 1.5, ALU.mult, ALU.add),
                                   lambda: nc.vector.tensor_tensor(rs[:], rs[:], rs_t[:], ALU.mult))):
                f().then_inc(s_rs, 1)
                dve.wait_ge(s_rs, 5 * n + a + 1)

        def sums_of_squares(act, src, junk_ap, n, ready=None):
            for t in range(NT):
                if ready:
                    act.wait_ge(ready[0], ready[1] * (t + 1))
                nc.scalar.activation(junk_ap, src[:, t], ACT.Square, accum_out=ss[:, t:t + 1]).then_inc(s_ss, 1)
                act.wait_ge(s_ss, n * NT + t + 1)
            act.wait_ge(s_ms, n + 1)
            nc.scalar.activation(rs[:], ss[:], ACT.Sqrt).then_inc(s_rt, 1)

        block = ctx.enter_context(nc.Block())

        def mm3(out_ap, lh, ll, rh, rl, first, last):
            nc.tensor.matmul(out_ap, ll, rh, start=first, stop=False)
            nc.tensor.matmul(out_ap, lh, rl, start=False, stop=False)
            return nc.tensor.matmul(out_ap, lh, rh, start=False, stop=last)

        def sp_phase_done(sp):
            sp.drain().then_inc(s_phase, 1)
            phases["sp"] += 1
            sp.wait_ge(s_phase, 5 * phases["sp"])

        def phase_done(eng, name):
            eng.drain().then_inc(s_phase, 1)
            phases[name] += 1
            eng.wait_ge(s_phase, 5 * phases[name])

        phases = dict(sp=0, pool=0, act=0, dve=0, pe=0)

        @block.sync
        def _(sp):
            for t in range(NT):
                sp.dma_start(xs[:, t], x[t * P:(t + 1) * P, :]).then_inc(s_x, 16)
            sp.dma_start(gmix_col[:], g_mix).then_inc(s_gcol, 16)
            sp.dma_start(wba_raw[:], w_ba).then_inc(s_ba, 16)
            sp.wait_ge(s_xt, 16)
            for c in range(2):
                sp.dma_start(wraw[:, c], wt[c]).then_inc(s_wraw[c], 16)
            with sp.Fori(0, (N_ABC - 2) // 2) as i:
                for u in range(2):
                    sp.wait_ge(s_wl, i * 2 + (u + 1))
                    sp.dma_start(wraw[:, u], wt[bass.ds(i * 2 + (u + 2), 1)].rearrange("a p k n -> (a p) k n")).then_inc(s_wraw[u], 16)

            sp.wait_ge(s_st[0], 16 * N_CH // 2)
            sp.wait_ge(s_st[1], 16 * N_CH // 2)
            sp_phase_done(sp)
            for dst, src in ((aw[:], a_ws_t), (a_bias[:], a_bs), (a_gbt[:], a_gb), (c_sel[:], sel), (c_relb[0:REL_BUCKETS], relb)):
                sp.dma_start(dst, src).then_inc(s_aload, 16)
            sp.dma_start(a_u[:], pt[ROW_AU:ROW_AU + NC, :].rearrange("(g p) t -> p g t", p=P)).then_inc(s_au, 16)
            sp.wait_ge(s_fr, 5)
            sp.dma_start(frs, c_fr[:]).then_inc(s_frd, 16)
            sp.wait_ge(s_ay, 2 * NH)
            sp.dma_start(ys[0:NC, :].rearrange("(g p) t -> p g t", p=P), a_y[:]).then_inc(s_ydma, 16)
            sp.wait_ge(s_frd, 16)
            sp.wait_ge(s_ydma, 16)
            sp_phase_done(sp)
            for h in range(NH):
                u = h % 2
                if h >= 2:
                    sp.wait_ge(s_pv, 8 * (h - 1))
                for dst, row in ((c_q, ROW_CQ), (c_k, ROW_CK)):
                    for g in range(3):
                        sp.dma_start(dst[:, u, g], pt[row + g * NC + h * HD:row + g * NC + (h + 1) * HD, :]).then_inc(s_cin[u], 16)
                at = 0
                for g in range(3):
                    n = BAND_COLS[g]
                    sp.dma_start(c_tab[:, u, BAND_AT[g]:BAND_AT[g] + n],
                                 bass.AP(tensor=frs.tensor, offset=(4 * g + h) * BIAS_LEN + at,
                                         ap=[[1, P], [1, n]])).then_inc(s_cin[u], 16)
                    at += n + P - 1
            for u in range(2):
                sp.wait_ge(s_yst[u], 32)
            sp_phase_done(sp)
            for dst, src in ((b_m[:], b_masks), (b_cw[:], conv_w), (b_hvt[:], b_hv), (b_ngt[:], b_ng)):
                sp.dma_start(dst, src).then_inc(s_bload, 16)
            for n in range(NCONV):
                if n >= 2:
                    sp.wait_ge(s_bconv, n - 1)
                sp.dma_start(b_raw[:, n % 2, 3:T + 3], pt[ROW_BQ + n * HD:ROW_BQ + (n + 1) * HD, :]).then_inc(s_braw[n % 2], 16)
            sp.wait_ge(s_su, 2 * NT + 1)
            sp.wait_ge(s_oev, 2 * NT + 1)
            sp.dma_start(b_z[:], pt[ROW_BZ:ROW_BZ + NC, :].rearrange("(h p) t -> p h t", p=P)).then_inc(s_zl, 16)
            sp.wait_ge(s_yb, 2 * NH)
            sp.dma_start(ys[NC:2 * NC, :].rearrange("(h p) t -> p h t", p=P), b_c[:, 0:NH]).then_inc(s_ydma, 16)
            sp.wait_ge(s_ydma, 32)
            sp_phase_done(sp)
            for br in range(3):
                if br:
                    sp.wait_ge(s_yl2, NH * br)
                sp.dma_start(y_raw[:], ys[br * NC:(br + 1) * NC, :].rearrange("(g p) t -> p g t", p=P)).then_inc(s_yl, 16)
                for n in range(NB):
                    m = br * NB + n
                    u = m % 2
                    if m >= 2:
                        sp.wait_ge(s_gl, m - 1)
                    sp.dma_start(g_raw[:, u], wt[N_ABC + m // 2, :, :, (m % 2) * P:(m % 2 + 1) * P]).then_inc(s_gr[u], 16)
                    sp.dma_start(br_raw[:, u], w_br[br, n]).then_inc(s_gr[u], 16)
            sp_phase_done(sp)
            for c in range(4):
                if c >= 2:
                    sp.wait_ge(s_wol, c - 1)
                sp.dma_start(wo_raw[:, c % 2], w_o[c]).then_inc(s_wor[c % 2], 16)
                if c == 1:
                    for dst, src in ((x2[:], x.rearrange("(t p) d -> p t d", p=P)), ):
                        sp.dma_start(dst, src).then_inc(s_x2l, 16)
                    for dst, src in ((gffn_col[:], g_ffn), (wr[:], w_r), (iot[:], iotas[:, 0:96]), (strict[:], iotas[:, 96:96 + P]),
                                     (tids[:], tok_ids)):
                        sp.dma_start(dst, src).then_inc(s_rc, 16)
            for t in range(NT):
                sp.wait_ge(s_xn2, t + 1)
                sp.dma_start(h2s[t * P:(t + 1) * P, :], xn2[:, t]).then_inc(s_x2d, 16)
            sp.wait_ge(s_x2d, 16 * NT)
            sp_phase_done(sp)
            nb = sp.value_load(bexp[0:1, NBLK:NBLK + 1], min_val=2, max_val=NBLK)

            def load_expert(b, chunks, peeled=False):
                e = sp.value_load(bexp[0:1, bass.ds(b, 1)], min_val=0, max_val=31)
                for c in chunks:
                    if not peeled:
                        sp.wait_ge(*((s_el13, b * 4 + (c - 3)) if c < 4 else (s_el2, b * 2 + (c - 5))))
                    w, k0, nk = ((w1, 0, 4), (w1, 4, 4), (w3, 0, 4), (w3, 4, 4), (w2, 0, 2), (w2, 2, 2))[c]
                    src = w[bass.ds(e, 1)].rearrange("a (k p) f -> p (a k) f", p=P)[:, k0:k0 + nk, :]
                    sp.dma_start(e_raw[:, c].rearrange("p (k f) -> p k f", k=nk), src).then_inc(s_er[c], 16)

            load_expert(0, range(4), True)
            sp.wait_ge(s_xb, 16)
            load_expert(0, range(4, 6), True)
            load_expert(1, range(4))
            with sp.Fori(1, NBLK - 1) as b:
                with sp.If(b < nb):
                    with sp.If(b + 1 < nb):
                        load_expert(b + 1, range(4))
                    load_expert(b, range(4, 6))
            sp_phase_done(sp)
            sp.dma_start(gfin[:], g_fin).then_inc(s_fx, 16)
            for t in range(NT):
                sp.dma_start(yg[:, t], ybs.rearrange("(a t p) d -> t p a d", a=2, p=P)[t]).then_inc(s_fg[t], 16)
            for t in range(NT):
                sp.wait_ge(s_fo, t + 1)
                sp.dma_start(out[t * P:(t + 1) * P, :], x3[:, t]).then_inc(s_out, 16)
            sp.wait_ge(s_out, 16 * NT)

        @block.gpsimd
        def _(pool):
            pool.memset(ident[:], 0.0).then_inc(s_cst, 1)
            pool.wait_ge(s_cst, 1)
            pool.affine_select(out=ident[:], in_=ident[:], compare_op=ALU.not_equal, fill=1.0, base=0,
                               pattern=[[-1, P]], channel_multiplier=1).then_inc(s_cst, 1)
            pool.memset(ones[:], 1.0).then_inc(s_cst, 1)
            with pool.Fori(0, N_CH // 2) as i:
                for u in range(2):
                    pool.wait_ge(s_ev, (i * 2 + (u + N_TOK + 1)) * 4)
                    pool.dma_start(pt[bass.ds((i * 2 + u) * CW, CW), :].rearrange("(a p) t -> p a t", p=P),
                                   stage[:, u]).then_inc(s_st[u], 16)
            phase_done(pool, "pool")
            pool.memset(a_one[:], 1.0).then_inc(s_amask, 1)
            pool.wait_ge(s_aload, 16 * 5)
            pool.memset(c_relb[REL_BUCKETS:REL_BUCKETS + 1, :], 1.0).then_inc(s_amask, 1)
            pool.wait_ge(s_amask, 2)
            pool.affine_select(out=aw[:], in_=aw[:], compare_op=ALU.is_ge, fill=0.0, base=0,
                               pattern=[[0, NH], [1, P]], channel_multiplier=-1).then_inc(s_amask, 1)
            phase_done(pool, "pool")
            cp = Chain(pool, s_cp)
            with pool.Fori(0, NH // 2) as i:
                cp.enter(i, 16)
                for j in range(16):
                    (n1, n2, n3), (o1, o2, o3), w = widths(j % 8)
                    lg = c_lg[:, j % 3]
                    pool.wait_ge(s_ex, i * 16 + (j + 1))
                    cp.link(pool.tensor_tensor(lg[:, w - n2 * P:w], lg[:, w - n2 * P:w], lg[:, o2:o2 + n2 * P], ALU.add))
                    pool.tensor_tensor(lg[:, w - n1 * P:w], lg[:, w - n1 * P:w], lg[:, o1:o1 + n1 * P], ALU.add).then_inc(s_pa, 1)
                cp.leave(NH // 2)
            phase_done(pool, "pool")
            for h in cleared:
                pool.sem_clear(h)
            for u in range(2):
                pool.memset(b_raw[:, u, 0:3], 0.0).then_inc(s_bpad, 1)
            with pool.Fori(0, NT // 2) as i:
                pool.wait_ge(s_bset, 1)
                for u in range(2):
                    pool.wait_ge(s_su, i * 4 + 1)
                    pool.wait_ge(s_oev, i * 4 + 1)
                    pool.tensor_copy(kqv[:, u], b_c[:, :, bass.ds(i * (2 * P) + u * P, P)]).then_inc(s_pk, 1)
                    pool.tensor_copy(cur[:, u], PSC[:, bass.ds(i * 2 + u, 1), :].rearrange("p a n -> p (a n)")).then_inc(s_pk, 1)
                    if u:
                        pool.wait_ge(s_p1, i * 16 + 8)
                    pool.tensor_copy(bcs[:], SM[:, bass.ds(i * 2 + u, 1), :].rearrange("p a (n b) -> p (a n) b", b=1)
                                     .to_broadcast([P, 16, P])).then_inc(s_pk, 1)
                for l in range(LEVELS):
                    for u in range(2):
                        if l == 0:
                            pool.wait_ge(s_lt, i * 2 + (u + 1))
                        if l >= 2:
                            pool.wait_ge(s_pp, i * 12 + (2 * (l - 2) + u + 1))
                        pool.tensor_tensor(CT[:, u, l % 2], LT[:, u], bheads(b_m[:, 4 + l]), ALU.mult).then_inc(s_ct, 1)
            phase_done(pool, "pool")
            phase_done(pool, "pool")
            pool.memset(zer[:], NO_ROW).then_inc(s_rtz, 1)
            pool.wait_ge(s_rtz, 1)
            pool.dma_start(rts.rearrange("(p b) a -> p (b a)", p=P), zer[:]).then_inc(s_rtc, 16)
            pool.wait_ge(s_rtc, 16)
            pool.wait_ge(s_rd1, ROUTER_STEPS)
            for t in range(NT):
                for a in range(2):
                    pool.indirect_dma_start(out=rts, out_offset=bass.IndirectOffsetOnAxis(ap=place[:, t, a:a + 1], axis=0),
                                            in_=tids[:, a, t:t + 1], in_offset=None).then_inc(s_rts, 16)
            pool.wait_ge(s_rts, 16 * 2 * NT)
            phase_done(pool, "pool")
            pool.dma_start(rasg[:], rts.rearrange("(p b) a -> p (b a)", p=P)).then_inc(s_rtl, 16)
            pool.memset(zero[:], 0.0)
            pool.memset(xb[:], 0.0).then_inc(s_rix, 1)
            pool.wait_ge(s_rix, 1)
            pool.wait_ge(s_rtl, 16)
            pool.tensor_scalar(rtok[:], rasg[:], float(T), float(T), ALU.is_ge, ALU.mult).then_inc(s_rix, 1)
            pool.wait_ge(s_rix, 2)
            pool.tensor_tensor(rtok[:], rasg[:], rtok[:], ALU.subtract).then_inc(s_rix, 1)
            pool.wait_ge(s_rix, 3)
            nb = pool.value_load(bexp[0:1, NBLK:NBLK + 1], min_val=2, max_val=NBLK)

            last_token, last_assignment = pool.to_reg(T - 1), pool.to_reg(2 * T - 1)

            def gather(b):
                pool.tensor_copy(bidx[:], rtok_all[:, bass.ds(b, 1)])
                pool.drain()
                pool.indirect_dma_start(out=xb[:], out_offset=None, in_=h2s,
                                        in_offset=bass.IndirectOffsetOnAxis(ap=bidx[:], axis=0),
                                        bounds_check=last_token, oob_is_err=False).then_inc(s_xb, 16)

            def move_rows(b, first=False):
                pool.wait_ge(s_xb, b * 16 + 16)
                if not first:
                    pool.wait_ge(s_tx, b * 2)
                pool.tensor_tensor(xr[:], xb[:], zero[:].to_broadcast([P, D]), ALU.add).then_inc(s_xr, 1)
                pool.wait_ge(s_xr, b + 1)

            def store(b, first=False):
                if not first:
                    pool.wait_ge(s_ys, b * 16)
                pool.wait_ge(s_ye, b * 2 + 2)
                pool.tensor_copy(aidx[:], rasg[:, bass.ds(b, 1)])
                pool.drain()
                pool.indirect_dma_start(out=ybs, out_offset=bass.IndirectOffsetOnAxis(ap=aidx[:], axis=0), in_=yb[:],
                                        in_offset=None, bounds_check=last_assignment, oob_is_err=False).then_inc(s_ys, 16)

            gather(0)
            move_rows(0, True)
            gather(1)
            move_rows(1)
            gather(2)
            move_rows(2)
            with pool.If(nb > 3):
                gather(3)
            store(0, True)
            with pool.Fori(2, NBLK - 1) as b:
                with pool.If(b < nb):
                    with pool.If(b + 1 < nb):
                        move_rows(b + 1)
                    with pool.If(b + 2 < nb):
                        gather(b + 2)
                    store(b - 1)
                    with pool.If(b + 1 >= nb):
                        store(b)
                        pool.wait_ge(s_ys, b * 16 + 16)
            phase_done(pool, "pool")
        @block.scalar
        def _(act):
            act.wait_ge(s_x, 16 * NT)
            sums_of_squares(act, xs, junk[:], 0)
            act.wait_ge(s_gcol, 16)
            n = 0
            for t in range(NT):
                for q in range(2):
                    act.wait_ge(s_xt, n + 1)
                    for j in range(4):
                        k = 4 * q + j
                        ins = nc.scalar.activation(hT_h[:, k, t * P:(t + 1) * P], ps[n % 4][:, j * P:(j + 1) * P],
                                                   ACT.Copy, scale=gmix_col[:, k:k + 1])
                    ins.then_inc(s_hh, 1)
                    n += 1
            act.wait_ge(s_ba, 16)
            nc.scalar.copy(wba_h[:], wba_raw[:]).then_inc(s_bah, 1)

            def split_high(u, count, n_wait):
                act.wait_ge(s_wraw[u], count)
                if n_wait is not None:
                    act.wait_ge(s_grp, n_wait)
                nc.scalar.copy(w_h[:, u], wraw[:, u]).then_inc(s_wh, 1)

            def evacuate_tok(c, u):
                for g in range(4):
                    act.wait_ge(s_grp, c * 4 + (g + 1))
                    nc.scalar.copy(tokv[:, 2 * g:2 * g + 2, bass.ds(c * CW, CW)],
                                   ps[g][:].rearrange("p (a n) -> p a n", a=2)).then_inc(s_ev, 1)

            def evacuate_ch(i, u, chunk, turned=False):
                act.wait_ge(s_st[u], i * 16)
                for g in range(4):
                    o = stage[:, u, g // 2, (g % 2) * HALF:(g % 2 + 1) * HALF].rearrange("p (a n) -> p a n", a=4)
                    act.wait_ge(s_grp, chunk * 4 + (g + 1))
                    nc.scalar.copy(o, banks4(g)[:, :, ::-1] if turned else banks4(g)).then_inc(s_ev, 1)

            split_high(0, 16, None)
            split_high(1, 16, None)
            for c in range(N_TOK):
                evacuate_tok(c, c % 2)
                split_high(c % 2, 16 * (c // 2 + 2), 4 * (c + 1))
            for u in range(2):
                for g in range(4):
                    act.wait_ge(s_grp, (N_TOK + u) * 4 + (g + 1))
                    nc.scalar.copy(stage[:, u, g // 2, (g % 2) * HALF:(g % 2 + 1) * HALF], ps[g][:]).then_inc(s_ev, 1)
                split_high(u, 16 * (N_TOK // 2 + 2), 4 * (N_TOK + u + 1))
            q_from, q_to = ROW_CQ // (2 * CW), ROW_CK // (2 * CW)
            for i0, i1 in ((1, q_from), (q_from, q_to), (q_to, N_CH // 2 - 1)):
                with act.Fori(i0, i1) as i:
                    for u in range(2):
                        evacuate_ch(i, u, i * 2 + (N_TOK + u), i0 == q_from)
                        split_high(u, (i + (N_TOK // 2 + 2)) * 16, (i * 2 + (N_TOK + u + 1)) * 4)
            for u in range(2):
                evacuate_ch(N_CH // 2 - 1, u, N_CH - 2 + N_TOK + u)
            act.wait_ge(s_grp, 4 * N_ABC + 1)
            nc.scalar.copy(ba[:], ps[4][:, 0:NT * 8].rearrange("p (t n) -> p t n", n=8)).then_inc(s_ev, 1)
            phase_done(act, "act")
            ca = Chain(act, s_ca)
            for t in range(NT):
                nc.scalar.activation(tokv[:, t, 0:NC], tokv[:, t, 0:NC], ACT.Gelu_apprx_tanh,
                                     accum_out=a_sum[:, t:t + 1]).then_inc(s_ag, 1)
            act.wait_ge(s_au, 16)
            for g in range(NH):
                nc.scalar.activation(a_u[:, g], a_u[:, g], ACT.Gelu_apprx_tanh).then_inc(s_aug, 1)
            act.wait_ge(s_amu, 1)
            for t in range(NT):
                ca.link(nc.scalar.activation(a_junk[:], tokv[:, t, 0:NC], ACT.Square, bias=a_sum[:, t:t + 1],
                                             accum_out=a_sq[:, t:t + 1]))
            act.wait_ge(s_avs, 1)
            nc.scalar.activation(a_sq[:], a_sq[:], ACT.Sqrt).then_inc(s_art, 1)
            phase_done(act, "act")
            with act.Fori(0, NH // 2) as i:
                def exponentials(j):
                    w = widths(j % 8)[2]
                    act.wait_ge(s_mx, i * 16 + (j + 1))
                    nc.scalar.activation(c_lg[:, j % 3, 0:w], c_lg[:, j % 3, 0:w], ACT.Exp, bias=c_st[:, j % 4, 1:2],
                                         accum_out=c_st[:, j % 4, 2:3]).then_inc(s_ex, 1)

                def rows_scaled(j):
                    act.wait_ge(s_pv, i * 16 + (j + 1))
                    act.wait_ge(s_rd, i * 16 + (j + 1))
                    nc.scalar.activation(c_rows[:, j // 8, j % 8], ps[6][:, 0:HD], ACT.Copy,
                                         scale=c_st[:, j % 4, 3:4]).then_inc(s_yc, 1)

                def rows_turned(u, r):
                    act.wait_ge(s_yt, i * 4 + (2 * u + r + 1))
                    nc.scalar.copy(c_yt[:, u, r * HALF:(r + 1) * HALF].rearrange("p (a n) -> p a n", a=4),
                                   banks4(7)[:, :, ::-1]).then_inc(s_yo, 1)
                    if r == 1:
                        act.wait_ge(s_yo, i * 4 + (2 * u + 2))
                        act.dma_start(ys[bass.ds(i * (2 * HD) + (2 * NC + u * HD), HD), :], c_yt[:, u]).then_inc(s_yst[u], 16)

                exponentials(0)
                exponentials(1)
                for j in range(16):
                    if j < 14:
                        exponentials(j + 2)
                    if j in (9, 10):
                        rows_turned(0, j - 9)
                    if j:
                        rows_scaled(j - 1)
                    if j >= 2:
                        act.wait_ge(s_pv, i * 16 + (j - 1))
                    act.wait_ge(s_tp, i * 16 + (j + 1))
                    nc.scalar.copy(c_pt[:, j % 2, 0:(j % 8 + 1) * P],
                                   psum[:, 4 * HALF:4 * HALF + (j % 8 + 1) * P]).then_inc(s_pt2, 1)
                rows_scaled(15)
                for r in range(2):
                    rows_turned(1, r)
                for u in range(2):
                    act.wait_ge(s_yst[u], i * 16 + 16)
            phase_done(act, "act")
            for n in range(NCONV):
                act.wait_ge(s_bconv, n + 1)
                nc.scalar.activation(b_c[:, n], b_c[:, n], ACT.Silu).then_inc(s_bsilu, 1)
                if n < NQ:
                    act.wait_ge(s_bsilu, n + 1)
                    if n >= 2:
                        act.wait_ge(s_bss, n - 1)
                    nc.scalar.activation(b_sq[:, n % 2], b_c[:, n], ACT.Square).then_inc(s_bsq, 1)
            act.wait_ge(s_bload, 64)
            nc.scalar.activation(eb[:], ba[:, :, 0:NH], ACT.Exp, scale=-1.0).then_inc(s_bn, 1)
            nc.scalar.activation(ea[:], b_hvt[:, 0], ACT.Exp).then_inc(s_bn, 1)
            act.wait_ge(s_bm, 1)
            nc.scalar.activation(xn[:], xn[:], ACT.Exp).then_inc(s_bn, 1)
            act.wait_ge(s_bm, 2)
            nc.scalar.activation(xl[:], xu[:], ACT.Ln).then_inc(s_bn, 1)
            act.wait_ge(s_bm, 4)
            nc.scalar.activation(qr[:], qs[:], ACT.Ln).then_inc(s_bn, 1)
            act.wait_ge(s_bn, 5)
            nc.scalar.activation(qr[:], qr[:], ACT.Exp, scale=-0.5).then_inc(s_bn, 1)
            act.wait_ge(s_bm, 5)
            nc.scalar.activation(eall[:], gall[:], ACT.Exp).then_inc(s_bn, 1)
            act.sem_inc(s_oev, 1)
            with act.Fori(0, NT // 2) as i:
                for u in range(2):
                    act.wait_ge(s_dm, i * 2 + (u + 1))
                    nc.scalar.activation(dE[:, u], dE[:, u], ACT.Exp).then_inc(s_de, 1)
                    act.wait_ge(s_pk, i * 6 + (3 * u + 2))
                    act.wait_ge(s_p1, i * 16 + (8 * u + 7))
                    for h in range(NH):
                        nc.scalar.activation(kbg[:, u, h], banks4(6)[:, h], ACT.Copy, scale=cur[:, u, 12 + h:13 + h])
                        nc.scalar.activation(kdec[:, u, h], banks4(6)[:, h], ACT.Copy, scale=cur[:, u, 16 + h:17 + h])
                    act.wait_ge(s_p1, i * 16 + (8 * u + 8))
                    for h in range(NH):
                        ins = nc.scalar.activation(vb[:, u, h], banks4(7)[:, h], ACT.Copy, scale=cur[:, u, 8 + h:9 + h])
                    ins.then_inc(s_a1, 1)
                for l in range(LEVELS):
                    for u in range(2):
                        act.wait_ge(s_pp, i * 12 + (2 * l + u + 1))
                        nc.scalar.copy(dP[:, u], banks4(3 * u)).then_inc(s_ps, 1)
                for u in range(2):
                    act.wait_ge(s_w, i * 2 + (u + 1))
                    nc.scalar.mul(wTn[:, u], banks4(3 * u), -1.0).then_inc(s_wn, 1)
                for c in range(4):
                    u, rows = c // 2, slice(CHUNK * (c % 2), CHUNK * (c % 2 + 1))
                    act.wait_ge(s_v, i * 4 + (c + 1))
                    nc.scalar.copy(vn[rows, c % 2], banks4(6)[rows]).then_inc(s_vn, 1)
                    act.wait_ge(s_o, i * 4 + (c + 1))
                    nc.scalar.copy(b_c[:, NQ:NCONV, bass.ds(i * (2 * P) + c * CHUNK, CHUNK)],
                                   ps[7][:, 0:NH * CHUNK].rearrange("p (h n) -> p h n", h=NH)).then_inc(s_oev, 1)
            act.wait_ge(s_oev, 2 * NT + 1)
            for h in range(NH):
                nc.scalar.activation(b_c[:, NH + h], b_c[:, NQ + h], ACT.Square).then_inc(s_oq, 1)
            act.wait_ge(s_zl, 16)
            for h in range(NH):
                nc.scalar.activation(b_z[:, h], b_z[:, h], ACT.Silu).then_inc(s_zs, 1)
            for n in range(2 * NH):
                act.wait_ge(s_oa, n + 1)
                if n >= 2:
                    act.wait_ge(s_yb, n - 1)
                ca.link(nc.scalar.activation(o_y[:, n % 2], o_a[:, n % 2], ACT.Ln))
                nc.scalar.activation(o_y[:, n % 2], o_y[:, n % 2], ACT.Exp, scale=-0.5).then_inc(s_ol, 1)
            phase_done(act, "act")
            def gate_high(m, u):
                act.wait_ge(s_gr[u], (m - u) * 16 + 32)
                if not (isinstance(m, int) and m < 2):
                    act.wait_ge(s_pm, m * 4 - 4)
                nc.scalar.copy(g_h[:, u], g_raw[:, u])
                nc.scalar.copy(br_h[:, u], br_raw[:, u]).then_inc(s_gh, 1)

            def gate(m, u):
                for h in range(2):
                    act.wait_ge(s_pm, m * 4 + (2 * h + 1))
                    if not (isinstance(m, int) and m < 1):
                        act.wait_ge(s_mg, m * 2 + (h - 1))
                    nc.scalar.activation(sig[:, h], ps[4 * u + 2 * h], ACT.Sigmoid).then_inc(s_sg, 1)

            for br in range(3):
                m0 = br * NB
                act.wait_ge(s_yl, 16 * (br + 1))
                if br:
                    act.wait_ge(s_pm, 4 * m0)
                for k in range(NH):
                    nc.scalar.copy(y_h[:, k], y_raw[:, k]).then_inc(s_yh, 1)
                if br == 0:
                    gate_high(0, 0)
                gate_high(m0 + 1, 1)
                gate(m0, 0)
                gate_high(m0 + 2, 0)
                gate(m0 + 1, 1)
                with act.Fori(1, NB // 2 - 1) as i:
                    for u in range(2):
                        gate_high(i * 2 + (m0 + u + 1), 1 - u)
                        gate(i * 2 + (m0 + u), u)
                gate_high(m0 + 7, 1)
                gate(m0 + 6, 0)
                if br < 2:
                    gate_high(m0 + 8, 0)
                gate(m0 + 7, 1)
            phase_done(act, "act")
            for k in range(KD):
                nc.scalar.copy(m_h[:, k], merged[:, k]).then_inc(s_mh, 1)
            for c in range(4):
                act.wait_ge(s_wor[c % 2], 16 * (c // 2 + 1))
                if c >= 2:
                    act.wait_ge(s_po, 4 * (c - 1))
                nc.scalar.copy(wo_h[:, c % 2], wo_raw[:, c % 2]).then_inc(s_woh, 1)
            act.wait_ge(s_x2, 4 * 4)
            sums_of_squares(act, x2, junk2[:], 1)
            act.wait_ge(s_rc, 16 * 5)
            n = 0
            for t in range(NT):
                for q in range(2):
                    act.wait_ge(s_t2, n + 1)
                    for j in range(4):
                        k = 4 * q + j
                        ins = nc.scalar.activation(h2T[:, k, t * P:(t + 1) * P], ps[n % 4][:, j * P:(j + 1) * P],
                                                   ACT.Copy, scale=gffn_col[:, k:k + 1])
                    ins.then_inc(s_h2, 1)
                    n += 1
            act.wait_ge(s_rd1, GROUP_SHIFTED)
            nc.scalar.activation(gd[:], gd[:], ACT.Exp).then_inc(s_ra, 1)
            act.wait_ge(s_rd1, SECOND_SHIFTED)
            nc.scalar.activation(m2[:], m2[:], ACT.Exp).then_inc(s_ra, 1)
            phase_done(act, "act")
            nb = act.value_load(bexp[0:1, NBLK:NBLK + 1], min_val=2, max_val=NBLK)

            def high(b, c, peeled):
                act.wait_ge(s_er[c], b * 16 + 16)
                if not peeled:
                    if c < 4:
                        act.wait_ge(s_e13, b * 4 + (c - 3))
                    else:
                        act.wait_ge(s_e2, b * 2 + (c - 5))
                nc.scalar.copy(e_h[:, c], e_raw[:, c]).then_inc(s_eh13 if c < 4 else s_eh2, 1)

            def rows_high(b):
                for r in range(2):
                    act.wait_ge(s_tx, b * 2 + (r + 1))
                    for j in range(4):
                        k = 4 * r + j
                        ins = nc.scalar.activation(xT_h[:, k], ps[r][:, j * P:(j + 1) * P], ACT.Copy, scale=gffn_col[:, k:k + 1])
                    ins.then_inc(s_xh, 1)

            def silu(b):
                act.wait_ge(s_e13, b * 4 + 2)
                if not (isinstance(b, int) and b == 0):
                    act.wait_ge(s_hd, b)
                nc.scalar.activation(sg[:], ps[2], ACT.Silu).then_inc(s_si, 1)

            def hidden_high(b):
                act.wait_ge(s_th, b + 1)
                nc.scalar.copy(hT2_h[:], banks4(6)).then_inc(s_hh2, 1)

            def rows_out(b, first):
                if not first:
                    act.wait_ge(s_ys, b * 16)
                for r in range(2):
                    act.wait_ge(s_e2, b * 2 + 2)
                    nc.scalar.copy(yb[:, r * HALF:(r + 1) * HALF], ps[4 + r]).then_inc(s_ye, 1)

            for c in range(4):
                high(0, c, True)
            rows_high(0)
            for c in range(3):
                high(1, c, False)
            silu(0)
            rows_high(1)
            high(1, 3, False)
            hidden_high(0)
            for c in range(4, 6):
                high(0, c, True)

            def act_block(b, first):
                with act.If(b + 1 < nb):
                    for c in range(3):
                        high(b + 1, c, False)
                silu(b)
                with act.If(b + 1 < nb):
                    rows_high(b + 1)
                    high(b + 1, 3, False)
                rows_out(b - 1, first)
                hidden_high(b)
                for c in range(4, 6):
                    high(b, c, False)

            act_block(1, True)
            with act.Fori(2, NBLK - 1) as b:
                with act.If(b < nb):
                    act_block(b, False)
                    with act.If(b + 1 >= nb):
                        rows_out(b, False)
            phase_done(act, "act")
            sums_of_squares(act, x3, fjunk[:], 2, ready=(s_f3, 1))

        @block.vector
        def _(dve):
            inverse_rms(dve, 0)
            for t in range(NT):
                nc.vector.tensor_scalar(xs[:, t], xs[:, t], rs[:, t:t + 1], None, ALU.mult).then_inc(s_xn, 1)
            n = 0
            for t in range(NT):
                for q in range(2):
                    dve.wait_ge(s_hh, n + 1)
                    for j in range(4):
                        k = 4 * q + j
                        ins = nc.vector.scalar_tensor_tensor(
                            hT_l[:, k, t * P:(t + 1) * P], ps[n % 4][:, j * P:(j + 1) * P], gmix_col[:, k:k + 1],
                            hT_h[:, k, t * P:(t + 1) * P].bitcast(F32), ALU.mult, ALU.subtract)
                    ins.then_inc(s_hl, 1)
                    n += 1
            dve.wait_ge(s_bah, 1)
            nc.vector.tensor_tensor(wba_l[:], wba_raw[:], wba_h[:].bitcast(F32), ALU.subtract).then_inc(s_bah, 1)
            for c in range(2):
                dve.wait_ge(s_wh, c + 1)
                nc.vector.tensor_tensor(w_l[:, c], wraw[:, c], w_h[:, c].bitcast(F32), ALU.subtract).then_inc(s_wl, 1)
            with dve.Fori(1, N_ABC // 2) as i:
                for u in range(2):
                    dve.wait_ge(s_wh, i * 2 + (u + 1))
                    nc.vector.tensor_tensor(w_l[:, u], wraw[:, u], w_h[:, u].bitcast(F32), ALU.subtract).then_inc(s_wl, 1)
            phase_done(dve, "dve")
            cd = Chain(dve, s_cd)
            for b in range(5):
                w = min(HALF, BIAS_LEN - b * HALF)
                dve.wait_ge(s_frmm, b + 1)
                nc.vector.tensor_copy(c_fr[:, b * HALF:b * HALF + w], ps[b][0:12, 0:w]).then_inc(s_fr, 1)
            dve.wait_ge(s_ag, NT)
            nc.vector.tensor_scalar(a_sum[:], a_sum[:], -1.0 / NC, None, ALU.mult).then_inc(s_amu, 1)
            dve.wait_ge(s_ca, NT)
            nc.vector.tensor_scalar(a_sq[:], a_sq[:], 1.0 / NC, EPS, ALU.mult, ALU.add).then_inc(s_avs, 1)
            dve.wait_ge(s_art, 1)
            cd.link(nc.vector.reciprocal(a_sq[:], a_sq[:]))
            dve.wait_ge(s_aload, 16 * 5)
            for t in range(NT):
                v = tokv[:, t, 0:NC]
                cd.link(nc.vector.tensor_scalar(v, v, a_sum[:, t:t + 1], a_sq[:, t:t + 1], ALU.add, ALU.mult))
                cd.link(nc.vector.tensor_tensor(v, v, a_gbt[:, 0], ALU.mult))
                nc.vector.tensor_tensor(v, v, a_gbt[:, 1], ALU.add).then_inc(s_an, 1)
            dve.wait_ge(s_aug, NH)
            for n in range(2 * NH):
                g, q = n // 2, n % 2
                dve.wait_ge(s_asv, n + 1)
                nc.vector.tensor_tensor(a_y[:, g, q * HALF:(q + 1) * HALF], ps[n % 4], a_u[:, g, q * HALF:(q + 1) * HALF],
                                        ALU.mult).then_inc(s_ay, 1)
            phase_done(dve, "dve")
            with dve.Fori(0, NH // 2) as i:
                cd.enter(i, 16)
                for j in range(16):
                    n, off, w = widths(j % 8)
                    u = j // 8
                    if j % 8 == 0:
                        dve.wait_ge(s_cin[u], i * 144 + 144)
                    dve.wait_ge(s_lg, i * 16 + (j + 1))
                    if j >= 3:
                        dve.wait_ge(s_tp, i * 16 + (j - 2))
                    for g in range(3):
                        end = BAND_AT[g] + BAND_COLS[g]
                        ins = nc.vector.scalar_tensor_tensor(
                            c_lg[:, j % 3, off[g]:off[g] + n[g] * P], psum[:, off[g]:off[g] + n[g] * P], float(HD) ** -0.5,
                            c_tab[:, u, end - n[g] * P:end], ALU.mult, ALU.add)
                    ins.then_inc(s_lb, 1)
                    dve.wait_ge(s_lb, i * 16 + (j + 1))
                    cd.link(nc.vector.reduce_max(c_st[:, j % 4, 0:1], c_lg[:, j % 3, 0:w], AX))
                    if j >= 4:
                        dve.wait_ge(s_yc, i * 16 + (j - 3))
                    nc.vector.tensor_scalar(c_st[:, j % 4, 1:2], c_st[:, j % 4, 0:1], -1.0, None, ALU.mult).then_inc(s_mx, 1)
                    for k in ([j - 1] if j else []) + ([j] if j == 15 else []):
                        dve.wait_ge(s_ex, i * 16 + (k + 1))
                        nc.vector.reciprocal(c_st[:, k % 4, 3:4], c_st[:, k % 4, 2:3]).then_inc(s_rd, 1)
                cd.leave(NH // 2)
            phase_done(dve, "dve")
            nv = nc.vector
            dve.wait_ge(s_bload, 64)
            dve.wait_ge(s_bpad, 2)
            for n in range(NCONV):
                dve.wait_ge(s_braw[n % 2], 16 * (n // 2 + 1))
                raw = b_raw[:, n % 2]
                cd.link(nv.tensor_scalar(b_c[:, n], raw[:, 0:T], b_cw[:, n, 0:1], None, ALU.mult))
                cd.link(nv.scalar_tensor_tensor(b_c[:, n], raw[:, 1:T + 1], b_cw[:, n, 1:2], b_c[:, n], ALU.mult, ALU.add))
                cd.link(nv.scalar_tensor_tensor(b_c[:, n], raw[:, 2:T + 2], b_cw[:, n, 2:3], b_c[:, n], ALU.mult, ALU.add))
                nv.scalar_tensor_tensor(b_c[:, n], raw[:, 3:T + 3], b_cw[:, n, 3:4], b_c[:, n], ALU.mult, ALU.add).then_inc(s_bconv, 1)
            per_tok = lambda ap: ap.rearrange("p (a n) -> p a n", a=1).to_broadcast([P, NT, NH])
            cd.link(nv.tensor_tensor(xg[:], ba[:, :, NH:2 * NH], per_tok(b_hvt[:, 1]), ALU.add))
            cd.link(nv.tensor_scalar(xm[:], xg[:], 0.0, None, ALU.max))
            nv.scalar_tensor_tensor(xn[:], xm[:], -2.0, xg[:], ALU.mult, ALU.add).then_inc(s_bm, 1)
            dve.wait_ge(s_bn, 3)
            nv.tensor_scalar(xu[:], xn[:], 1.0, None, ALU.add).then_inc(s_bm, 1)
            dve.wait_ge(s_bm, 2)
            cd.link(nv.scalar_tensor_tensor(xc[:], xu[:], -1.0, xn[:], ALU.add, ALU.subtract))
            cd.link(nv.reciprocal(xg[:], xu[:]))
            cd.link(nv.tensor_tensor(xc[:], xc[:], xg[:], ALU.mult))
            dve.wait_ge(s_bn, 4)
            cd.link(nv.tensor_tensor(xl[:], xl[:], xm[:], ALU.add))
            cd.link(nv.tensor_tensor(xl[:], xl[:], xc[:], ALU.subtract))
            nv.scalar_tensor_tensor(SM[:, :, 0:NH], xl[:], -1.0, per_tok(ea[:]), ALU.mult, ALU.mult).then_inc(s_bm, 1)
            cd.link(nv.tensor_scalar(eb[:], eb[:], 1.0, None, ALU.add))
            beta = PSC[:, :, 8:12]
            cd.link(nv.reciprocal(beta, eb[:]))
            dve.wait_ge(s_bss, NQ)
            nv.tensor_scalar(qs[:], ps[7][:, 0:NT * NQ].rearrange("p (t n) -> p t n", n=NQ), EPS, None, ALU.add).then_inc(s_bm, 1)
            dve.wait_ge(s_bgc, 1)
            cd.link(nv.tensor_copy(gall[:], ps[6][:, 0:4 * NT * NH].rearrange("p (a t n) -> p a t n", a=4, n=NH)))
            cd.link(nv.tensor_copy(PSC[:, :, 0:4], gall[:, 0]))
            nv.tensor_tensor(gall[:, 1], gall[:, 1], gall[:, 0], ALU.subtract).then_inc(s_bm, 1)
            dve.wait_ge(s_bn, 6)
            cd.link(nv.tensor_tensor(qt_[:], qs[:], qr[:], ALU.mult))
            cd.link(nv.tensor_tensor(qt_[:], qt_[:], qr[:], ALU.mult))
            cd.link(nv.tensor_scalar(qt_[:], qt_[:], -0.5, 1.5, ALU.mult, ALU.add))
            cd.link(nv.tensor_tensor(qr[:], qr[:], qt_[:], ALU.mult))
            cd.link(nv.tensor_scalar(SM[:, :, 8:12], qr[:, :, 0:NH], float(HD) ** -0.5, None, ALU.mult))
            cd.link(nv.tensor_copy(PSC[:, :, 4:8], qr[:, :, NH:NQ]))
            cd.link(nv.tensor_tensor(SM[:, :, 4:8], qr[:, :, NH:NQ], beta, ALU.mult))
            dve.wait_ge(s_bn, 7)
            cd.link(nv.tensor_tensor(SM[:, :, 12:16], SM[:, :, 8:12], eall[:, 0], ALU.mult))
            cd.link(nv.tensor_tensor(PSC[:, :, 12:16], SM[:, :, 4:8], eall[:, 0], ALU.mult))
            cd.link(nv.tensor_tensor(PSC[:, :, 16:20], PSC[:, :, 4:8], eall[:, 1], ALU.mult))
            cd.link(nv.tensor_copy(PSC[:, :, 20:24], eall[:, 2]))
            cd.link(nv.tensor_copy(PSC[:, :, 24:28], eall[:, 3]))
            nv.memset(S[:], 0.0).then_inc(s_su, 1)
            nv.memset(vn[:], 0.0).then_inc(s_bini, 1)
            dve.wait_ge(s_bini, 1)
            dve.wait_ge(s_su, 1)
            nv.memset(b_mark[:], 0.0).then_inc(s_bset, 1)
            with dve.Fori(0, NT // 2) as i:
                cd.enter(i, 6)
                for u in range(2):
                    dve.wait_ge(s_pk, i * 6 + (3 * u + 2))
                    dve.wait_ge(s_p1, i * 16 + (8 * u + 1))
                    for h in range(NH):
                        ins = nv.tensor_scalar(dE[:, u, h], banks4(0)[:, h], cur[:, u, h:h + 1], 0.0, ALU.subtract, ALU.min)
                    ins.then_inc(s_dm, 1)
                    dve.wait_ge(s_de, i * 2 + (u + 1))
                    for h in range(NH):
                        ins = nv.scalar_tensor_tensor(dE[:, u, h], dE[:, u, h], cur[:, u, 4 + h:5 + h], U_INCL, ALU.mult, ALU.mult)
                    cd.link(ins)
                    dve.wait_ge(s_p1, i * 16 + (8 * u + 3))
                    cd.link(nv.tensor_tensor(AT[:, u], dE[:, u], banks4(1), ALU.mult))
                    nv.tensor_tensor(AT[:, u], AT[:, u], banks4(2), ALU.mult)
                    dve.wait_ge(s_p1, i * 16 + (8 * u + 5))
                    cd.link(nv.tensor_tensor(LT[:, u], dE[:, u], banks4(3), ALU.mult))
                    nv.tensor_tensor(LT[:, u], LT[:, u], banks4(4), ALU.mult).then_inc(s_lt, 1)
                    dve.wait_ge(s_p1, i * 16 + (8 * u + 6))
                    nv.tensor_tensor(qdec[:, u], kqv[:, u, 0:NH], banks4(5), ALU.mult).then_inc(s_qd, 1)
                for l in range(LEVELS):
                    for u in range(2):
                        dve.wait_ge(s_xy, i * 12 + (2 * l + u + 1))
                        if l == 0:
                            nv.tensor_tensor(dD[:, u], bheads(ident[:]), banks4(3 * u + 1), ALU.subtract)
                            nv.tensor_tensor(dR[:, u], bheads(ident[:]), banks4(3 * u + 2), ALU.subtract).then_inc(s_du, 1)
                        else:
                            if l < LEVELS - 1:
                                nv.tensor_tensor(dD[:, u], dD[:, u], banks4(3 * u + 1), ALU.subtract)
                            nv.tensor_tensor(dR[:, u], dR[:, u], banks4(3 * u + 2), ALU.subtract).then_inc(s_du, 1)
                for c in range(4):
                    dve.wait_ge(s_sm, i * 4 + (c + 1))
                    for h in range(NH):
                        ins = nv.scalar_tensor_tensor(S[:, h], S[:, h], cur[:, c // 2, 20 + 4 * (c % 2) + h:21 + 4 * (c % 2) + h],
                                                      banks4(c % 2)[:, h], ALU.mult, ALU.add)
                    ins.then_inc(s_su, 1)
                cd.leave(NT // 2)
            for n in range(2 * NH):
                h, cols = n // 2, slice((n % 2) * HALF, (n % 2 + 1) * HALF)
                y, t = o_y[:, n % 2], o_t[:, n % 2]
                if n == 0:
                    dve.wait_ge(s_oev, 2 * NT + 1)
                dve.wait_ge(s_om, n + 1)
                nv.tensor_scalar(o_a[:, n % 2], ps[n % 4], 1.0 / HD, EPS, ALU.mult, ALU.add).then_inc(s_oa, 1)
                dve.wait_ge(s_ol, n + 1)
                cd.link(nv.tensor_tensor(t, o_a[:, n % 2], y, ALU.mult))
                cd.link(nv.tensor_tensor(t, t, y, ALU.mult))
                cd.link(nv.tensor_scalar(t, t, -0.5, 1.5, ALU.mult, ALU.add))
                cd.link(nv.tensor_tensor(t, t, y, ALU.mult))
                cd.link(nv.scalar_tensor_tensor(t, t, b_ngt[:], b_c[:, NQ + h, cols], ALU.mult, ALU.mult))
                dve.wait_ge(s_zs, h + 1)
                nv.tensor_tensor(b_c[:, h, cols], t, b_z[:, h, cols], ALU.mult).then_inc(s_yb, 1)
            phase_done(dve, "dve")
            def gate_low(m, u):
                dve.wait_ge(s_gh, m + 1)
                nv.tensor_tensor(g_l[:, u], g_raw[:, u], g_h[:, u].bitcast(F32), ALU.subtract)
                nv.tensor_tensor(br_l[:, u], br_raw[:, u], br_h[:, u].bitcast(F32), ALU.subtract).then_inc(s_gl, 1)

            def merge(m, n, u, first):
                for h in range(2):
                    dve.wait_ge(s_sg, m * 2 + (h + 1))
                    dve.wait_ge(s_pm, m * 4 + (2 * h + 2))
                    o = merged[:, bass.ds(n, 1), h * HALF:(h + 1) * HALF].rearrange("p a t -> p (a t)")
                    if first:
                        nv.tensor_tensor(o, sig[:, h], ps[4 * u + 2 * h + 1], ALU.mult).then_inc(s_mg, 1)
                    else:
                        cd.link(nv.tensor_tensor(prod[:, h], sig[:, h], ps[4 * u + 2 * h + 1], ALU.mult))
                        nv.tensor_tensor(o, o, prod[:, h], ALU.add).then_inc(s_mg, 1)

            for br in range(3):
                m0 = br * NB
                for k in range(NH):
                    dve.wait_ge(s_yh, NH * br + k + 1)
                    nv.tensor_tensor(y_l[:, k], y_raw[:, k], y_h[:, k].bitcast(F32), ALU.subtract).then_inc(s_yl2, 1)
                if br == 0:
                    gate_low(0, 0)
                gate_low(m0 + 1, 1)
                merge(m0, 0, 0, br == 0)
                gate_low(m0 + 2, 0)
                merge(m0 + 1, 1, 1, br == 0)
                with dve.Fori(1, NB // 2 - 1) as i:
                    cd.enter(i, 0 if br == 0 else 4, first=1)
                    for u in range(2):
                        gate_low(i * 2 + (m0 + u + 1), 1 - u)
                        merge(i * 2 + (m0 + u), i * 2 + u, u, br == 0)
                    cd.leave(NB // 2 - 2)
                gate_low(m0 + 7, 1)
                merge(m0 + 6, 6, 0, br == 0)
                if br < 2:
                    gate_low(m0 + 8, 0)
                merge(m0 + 7, 7, 1, br == 0)
            phase_done(dve, "dve")
            def out_low(c):
                dve.wait_ge(s_woh, c + 1)
                nv.tensor_tensor(wo_l[:, c % 2], wo_raw[:, c % 2], wo_h[:, c % 2].bitcast(F32), ALU.subtract).then_inc(s_wol, 1)

            for k in range(KD):
                dve.wait_ge(s_mh, k + 1)
                nv.tensor_tensor(m_l[:, k], merged[:, k], m_h[:, k].bitcast(F32), ALU.subtract).then_inc(s_ml, 1)
            out_low(0)
            out_low(1)
            dve.wait_ge(s_x2l, 16)
            for c in range(4):
                for g in range(4):
                    o = x2[:, 2 * g:2 * g + 2, c * CW:(c + 1) * CW]
                    dve.wait_ge(s_po, 4 * c + g + 1)
                    nv.tensor_tensor(o, o, ps[g].rearrange("p (a n) -> p a n", a=2), ALU.add).then_inc(s_x2, 1)
                if c < 2:
                    out_low(c + 2)
            inverse_rms(dve, 1)
            for t in range(NT):
                nv.tensor_scalar(xn2[:, t], x2[:, t], rs[:, t:t + 1], None, ALU.mult).then_inc(s_xn2, 1)
            r = Chain(dve, s_rd1)
            wide = lambda ap, n: ap.to_broadcast([P, NT, n])
            row = lambda at, n: iot[:, at:at + n].rearrange("p (a n) -> p a n", a=1).to_broadcast([P, NT, n])
            r4 = lambda ap: ap.rearrange("p t (g e) -> p t g e", g=4)
            dve.wait_ge(s_rm, 1)
            dve.wait_ge(s_rc, 16 * 5)
            r.link(nv.tensor_copy(lg[:], ps[4][:, 0:NT * 36].rearrange("p (t n) -> p t n", n=36)))
            r.link(nv.reduce_max(gm[:], lg[:, :, 0:4], AX))
            r.link(nv.tensor_tensor(gd[:], lg[:, :, 0:4], wide(gm[:], 4), ALU.subtract))
            assert r.n == GROUP_SHIFTED

            def first_of(oh_ap, vals, mx, n):
                r.link(nv.tensor_tensor(cand[:, :, 0:n], vals, wide(mx, n), ALU.is_equal))
                r.link(nv.scalar_tensor_tensor(cand[:, :, 0:n], cand[:, :, 0:n], -1000.0, row(0, n), ALU.mult, ALU.add))
                r.link(nv.tensor_reduce(cm[:], cand[:, :, 0:n], axis=AX, op=ALU.min))
                r.link(nv.tensor_tensor(oh_ap, cand[:, :, 0:n], wide(cm[:], n), ALU.is_equal))

            first_of(goh[:], lg[:, :, 0:4], gm[:], 4)
            r.link(nv.tensor_tensor(selt[:], r4(lg[:, :, 4:36]), goh[:].rearrange("p t (g a) -> p t g a", a=1).to_broadcast([P, NT, 4, 8]), ALU.mult))
            r.link(nv.reduce_sum(sl[:], selt[:].rearrange("p t g e -> p t e g"), AX))
            r.link(nv.reduce_max(m1[:], sl[:], AX))
            first_of(oh[:, 0], sl[:], m1[:], 8)
            r.link(nv.scalar_tensor_tensor(sl[:], oh[:, 0], NEG, sl[:], ALU.mult, ALU.add))
            r.link(nv.reduce_max(m2[:], sl[:], AX))
            first_of(oh[:, 1], sl[:], m2[:], 8)
            r.link(nv.tensor_tensor(m2[:], m2[:], m1[:], ALU.subtract))
            assert r.n == SECOND_SHIFTED, r.n
            dve.wait_ge(s_ra, 1)
            r.link(nv.reduce_sum(gp[:], gd[:], AX))
            r.link(nv.reciprocal(gp[:], gp[:]))
            for a in range(2):
                r.link(nv.tensor_tensor(r4(O[:, a]), goh[:].rearrange("p t (g a) -> p t g a", a=1).to_broadcast([P, NT, 4, 8]),
                                        oh[:, a].rearrange("p t (a e) -> p t a e", a=1).to_broadcast([P, NT, 4, 8]), ALU.mult))
            r.link(nv.tensor_tensor(Osum[:], O[:, 0], O[:, 1], ALU.add))
            assert r.n == ONE_HOTS, r.n
            dve.wait_ge(s_ra, 2)
            r.link(nv.tensor_scalar(m1[:], m2[:], 1.0, None, ALU.add))
            r.link(nv.reciprocal(m1[:], m1[:]))
            r.link(nv.tensor_tensor(gates2[:, :, 0:1], gp[:], m1[:], ALU.mult))
            r.link(nv.tensor_tensor(gates2[:, :, 1:2], gates2[:, :, 0:1], m2[:], ALU.mult))
            dve.wait_ge(s_rk, 1)
            r.link(nv.tensor_copy(rank[:], ps[5][:, 0:NT * 32].rearrange("p (t n) -> p t n", n=32)))
            r.link(nv.tensor_scalar(padf[:], ps[5][:, NT * 32:NT * 32 + 32], float(P - 1), None, ALU.add))
            r.link(nv.tensor_copy(padi[:], padf[:]))
            r.link(nv.tensor_scalar(padi[:], padi[:], -P, None, ALU.bitwise_and))
            r.link(nv.tensor_copy(padf[:], padi[:]))
            r.link(nv.tensor_copy(pend[:, 0], padf[:]))
            for a in range(5):
                src, dst, d = pend[:, a % 2], pend[:, 1 - a % 2], 1 << a
                r.link(nv.tensor_copy(dst, src))
                r.link(nv.tensor_tensor(dst[:, d:32], src[:, d:32], src[:, 0:32 - d], ALU.add))
            ends = pend[:, 1]
            r.link(nv.tensor_tensor(padf[:], ends, padf[:], ALU.subtract))
            r.link(nv.tensor_tensor(rank[:], rank[:], padf[:].rearrange("p (a n) -> p a n", a=1).to_broadcast([P, NT, 32]), ALU.add))
            for a in range(2):
                r.link(nv.tensor_tensor(dtmp[:], O[:, a], rank[:], ALU.mult))
                r.link(nv.reduce_sum(dsum[:, :, a:a + 1], dtmp[:], AX))
            r.link(nv.tensor_copy(dest[:], dsum[:]))
            r.link(nv.tensor_scalar(ihi[:, 0], dest[:], P - 1, None, ALU.bitwise_and))
            r.link(nv.tensor_scalar(ihi[:, 1], dest[:], 7, None, ALU.logical_shift_right))
            r.link(nv.tensor_copy(fhi[:], ihi[:]))
            r.link(nv.scalar_tensor_tensor(dsum[:], fhi[:, 0], float(NBLK), fhi[:, 1], ALU.mult, ALU.add))
            r.link(nv.tensor_copy(place[:], dsum[:]))
            r.link(nv.tensor_tensor(bcmp[:], ends.rearrange("p (a n) -> p a n", a=1).to_broadcast([P, NBLK, 32]),
                                    iot[:, 32:32 + NBLK].rearrange("p (n a) -> p n a", a=1).to_broadcast([P, NBLK, 32]), ALU.is_le))
            r.link(nv.reduce_sum(bexf[:], bcmp[:], AX))
            r.link(nv.tensor_scalar(bexf[:], bexf[:], 31.0, None, ALU.min))
            dve.wait_ge(s_rm, 1)
            r.link(nv.tensor_scalar(bexf_n[:], ends[:, 31:32], 1.0 / P, None, ALU.mult))
            dve.wait_ge(s_x2d, 16 * NT)
            r.link(nv.tensor_copy(bexp[:, 0:NBLK], bexf[:]))
            r.link(nv.tensor_copy(bexp[:, NBLK:NBLK + 1], bexf_n[:]))
            assert r.n == ROUTER_STEPS, r.n
            phase_done(dve, "dve")
            nb = dve.value_load(bexp[0:1, NBLK:NBLK + 1], min_val=2, max_val=NBLK)

            def low(b, c):
                dve.wait_ge(*((s_eh13, b * 4 + (c + 1)) if c < 4 else (s_eh2, b * 2 + (c - 3))))
                nv.tensor_tensor(e_l[:, c], e_raw[:, c], e_h[:, c].bitcast(F32),
                                 ALU.subtract).then_inc(s_el13 if c < 4 else s_el2, 1)

            def rows_low(b):
                for r_ in range(2):
                    dve.wait_ge(s_xh, b * 2 + (r_ + 1))
                    for j in range(4):
                        k = 4 * r_ + j
                        ins = nv.scalar_tensor_tensor(xT_l[:, k], ps[r_][:, j * P:(j + 1) * P], gffn_col[:, k:k + 1],
                                                      xT_h[:, k].bitcast(F32), ALU.mult, ALU.subtract)
                    ins.then_inc(s_xl, 1)

            def hidden(b):
                dve.wait_ge(s_si, b + 1)
                dve.wait_ge(s_e13, b * 4 + 4)
                if not (isinstance(b, int) and b == 0):
                    dve.wait_ge(s_th, b)
                nv.tensor_tensor(hid[:], sg[:], ps[3], ALU.mult).then_inc(s_hd, 1)

            def hidden_low(b):
                dve.wait_ge(s_hh2, b + 1)
                nv.tensor_tensor(hT2_l[:], banks4(6), hT2_h[:].bitcast(F32), ALU.subtract).then_inc(s_hl2, 1)

            for c in range(4):
                low(0, c)
            rows_low(0)

            def dve_block(b, If):
                with If():
                    for c in range(3):
                        low(b + 1, c)
                hidden(b)
                with If():
                    rows_low(b + 1)
                    low(b + 1, 3)
                hidden_low(b)
                for c in range(4, 6):
                    low(b, c)

            dve_block(0, nullcontext)
            with dve.Fori(1, NBLK - 1) as b:
                with dve.If(b < nb):
                    dve_block(b, lambda: dve.If(b + 1 < nb))
            phase_done(dve, "dve")
            dve.wait_ge(s_fx, 16)
            for t in range(NT):
                dve.wait_ge(s_fg[t], 16)
                cd.link(nv.tensor_scalar(yg[:, t, 0], yg[:, t, 0], gates2[:, t, 0:1], None, ALU.mult))
                cd.link(nv.scalar_tensor_tensor(yg[:, t, 0], yg[:, t, 1], gates2[:, t, 1:2], yg[:, t, 0], ALU.mult, ALU.add))
                nv.tensor_tensor(x3[:, t], x3[:, t], yg[:, t, 0], ALU.add).then_inc(s_f3, 1)
            inverse_rms(dve, 2)
            for t in range(NT):
                nv.scalar_tensor_tensor(x3[:, t], x3[:, t], rs[:, t:t + 1], gfin[:], ALU.mult, ALU.mult).then_inc(s_fo, 1)

        @block.tensor
        def _(pe):
            pe.wait_ge(s_cst, 2)
            n = 0
            for t in range(NT):
                pe.wait_ge(s_xn, t + 1)
                for q in range(2):
                    if n >= 4:
                        pe.wait_ge(s_hl, n - 3)
                    for j in range(4):
                        k = 4 * q + j
                        ins = nc.tensor.transpose(ps[n % 4][:, j * P:(j + 1) * P], xs[:, t, k * P:(k + 1) * P], ident[:])
                    ins.then_inc(s_xt, 1)
                    n += 1
            pe.wait_ge(s_hl, 2 * NT)

            def tok_chunk(c):
                u = c % 2
                pe.wait_ge(s_wl, c + 1)
                for g in range(4):
                    if c >= 1:
                        pe.wait_ge(s_ev, 4 * (c - 1) + g + 1)
                    for a in range(2):
                        t = 2 * g + a
                        for k in range(KD):
                            ins = mm3(ps[g][:, a * CW:(a + 1) * CW], hT_h[:, k, t * P:(t + 1) * P], hT_l[:, k, t * P:(t + 1) * P],
                                      w_h[:, u, k], w_l[:, u, k], k == 0, k == KD - 1)
                    ins.then_inc(s_grp, 1)

            for c in range(N_TOK):
                tok_chunk(c)

            with pe.Fori(0, N_CH // 2) as i:
                for u in range(2):
                    pe.wait_ge(s_wl, i * 2 + (N_TOK + u + 1))
                    for g in range(4):
                        pe.wait_ge(s_ev, (i * 2 + (N_TOK + u - 1)) * 4 + (g + 1))
                        a, h = g // 2, g % 2
                        for k in range(KD):
                            ins = mm3(ps[g][:], w_h[:, u, k, a * P:(a + 1) * P], w_l[:, u, k, a * P:(a + 1) * P],
                                      hT_h[:, k, h * HALF:(h + 1) * HALF], hT_l[:, k, h * HALF:(h + 1) * HALF],
                                      k == 0, k == KD - 1)
                        ins.then_inc(s_grp, 1)
            pe.wait_ge(s_bah, 2)
            for t in range(NT):
                for k in range(KD):
                    ins = mm3(ps[4][:, t * 8:(t + 1) * 8], hT_h[:, k, t * P:(t + 1) * P], hT_l[:, k, t * P:(t + 1) * P],
                              wba_h[:, k], wba_l[:, k], k == 0, k == KD - 1)
            ins.then_inc(s_grp, 1)
            phase_done(pe, "pe")
            pe.wait_ge(s_aload, 16 * 5)
            pe.wait_ge(s_amask, 3)
            for b in range(5):
                w = min(HALF, BIAS_LEN - b * HALF)
                nc.tensor.matmul(ps[b][0:12, 0:w], c_relb[:], c_sel[:, b * HALF:b * HALF + w],
                                 start=True, stop=True).then_inc(s_frmm, 1)
            pe.wait_ge(s_fr, 5)
            for n in range(2 * NH):
                g, q = n // 2, n % 2
                pe.wait_ge(s_an, 4 * q + 4)
                if n >= 4:
                    pe.wait_ge(s_ay, n - 3)
                for a in range(4):
                    o = ps[n % 4][:, a * P:(a + 1) * P]
                    nc.tensor.matmul(o, tokv[:, 4 * q + a, g * HD:(g + 1) * HD], aw[:, g], start=True, stop=False)
                    ins = nc.tensor.matmul(o, a_one[:], a_bias[:, g * HD:(g + 1) * HD], start=False, stop=True)
                ins.then_inc(s_asv, 1)
            phase_done(pe, "pe")
            with pe.Fori(0, NH // 2) as i:
                def logits(j):
                    n, off, w = widths(j % 8)
                    qt, u = j % 8, j // 8
                    if qt == 0:
                        pe.wait_ge(s_cin[u], i * 144 + 144)
                    if j >= 1:
                        pe.wait_ge(s_lb, i * 16 + j)
                    for g in range(3):
                        at, key, left = off[g], (qt + 1 - n[g]) * P, n[g] * P
                        while left:
                            m = min(left, HALF - at % HALF)
                            ins = nc.tensor.matmul(psum[:, at:at + m], c_q[:, u, g, qt * P:(qt + 1) * P],
                                                   c_k[:, u, g, key:key + m], start=True, stop=True)
                            at, key, left = at + m, key + m, left - m
                    ins.then_inc(s_lg, 1)

                def values(j):
                    pe.wait_ge(s_pt2, i * 16 + (j + 1))
                    if j:
                        pe.wait_ge(s_yc, i * 16 + j)
                    for k in range(j % 8 + 1):
                        ins = nc.tensor.matmul(ps[6][:, 0:HD], c_pt[:, j % 2, k * P:(k + 1) * P],
                                               tokv[:, k, bass.ds(i * (2 * HD) + (NC + j // 8 * HD), HD)],
                                               start=k == 0, stop=k == j % 8)
                    ins.then_inc(s_pv, 1)

                def turn_rows(u, r):
                    pe.wait_ge(s_yc, i * 16 + (8 * u + 8))
                    if u + r:
                        pe.wait_ge(s_yo, i * 4 + (2 * u + r))
                    for a in range(4):
                        ins = nc.tensor.transpose(ps[7][:, a * P:(a + 1) * P], c_rows[:, u, 4 * r + a], ident[:])
                    ins.then_inc(s_yt, 1)

                logits(0)
                logits(1)
                for j in range(16):
                    if j < 14:
                        logits(j + 2)
                    if j in (9, 10):
                        turn_rows(0, j - 9)
                    if j:
                        values(j - 1)
                    w = widths(j % 8)[2]
                    pe.wait_ge(s_pa, i * 16 + (j + 1))
                    for k in range(j % 8 + 1):
                        ins = nc.tensor.transpose(psum[:, 4 * HALF + k * P:4 * HALF + (k + 1) * P],
                                                  c_lg[:, j % 3, w - (j % 8 + 1 - k) * P:w - (j % 8 - k) * P], ident[:])
                    ins.then_inc(s_tp, 1)
                values(15)
                for r in range(2):
                    turn_rows(1, r)
            phase_done(pe, "pe")
            for n in range(NQ):
                pe.wait_ge(s_bsq, n + 1)
                for t in range(NT):
                    ins = nc.tensor.matmul(ps[7][:, t * NQ + n:t * NQ + n + 1], b_sq[:, n % 2, t * P:(t + 1) * P], ones[:, 0:1],
                                           start=True, stop=True)
                ins.then_inc(s_bss, 1)
            pe.wait_ge(s_bm, 3)
            for n, m in enumerate((U_INCL, M_CHUNK, M_FIRST, M_SECOND)):
                ins = nc.tensor.matmul(ps[6][:, n * NT * NH:(n + 1) * NT * NH].rearrange("p (t n) -> p t n", n=NH), m, SM[:, :, 0:NH],
                                       start=True, stop=True)
            ins.then_inc(s_bgc, 1)
            mm = nc.tensor.matmul
            pe.wait_ge(s_bset, 1)
            with pe.Fori(0, NT // 2) as i:
                pe.wait_ge(s_su, i * 4 + 1)
                pe.wait_ge(s_oev, i * 4 + 1)
                for u in range(2):
                    pe.wait_ge(s_pk, i * 6 + (3 * u + 3))
                    if u:
                        pe.wait_ge(s_qd, i * 2 + 1)
                        pe.wait_ge(s_a1, i * 2 + 1)
                    q, k, v = (kqv[:, u, a * NH:(a + 1) * NH] for a in range(3))
                    for b, f in enumerate((
                            lambda o, h: mm(o, bcs[:, h], U_INCL, start=True, stop=True),
                            lambda o, h: mm(o, bcs[:, 8 + h], ident[:], start=True, stop=True),
                            lambda o, h: mm(o, k[:, h], q[:, h], start=True, stop=True),
                            lambda o, h: mm(o, bcs[:, 4 + h], ident[:], start=True, stop=True),
                            lambda o, h: mm(o, k[:, h], k[:, h], start=True, stop=True),
                            lambda o, h: mm(o, bcs[:, 12 + h], ident[:], start=True, stop=True),
                            lambda o, h: nc.tensor.transpose(o, k[:, h], ident[:]),
                            lambda o, h: nc.tensor.transpose(o, v[:, h], ident[:]))):
                        for h in range(NH):
                            ins = f(banks4(b)[:, h], h)
                        ins.then_inc(s_p1, 1)
                pe.wait_ge(s_qd, i * 2 + 2)
                for l in range(LEVELS):
                    for u in range(2):
                        pe.wait_ge(s_ct, i * 12 + (2 * l + u + 1))
                        if l:
                            pe.wait_ge(s_du, i * 12 + (2 * (l - 1) + u + 1))
                        for h in range(NH):
                            ins = mm(banks4(3 * u)[:, h], CT[:, u, l % 2, h], dD[:, u, h] if l else ident[:], start=True, stop=True)
                        ins.then_inc(s_pp, 1)
                    for u in range(2):
                        pe.wait_ge(s_ps, i * 12 + (2 * l + u + 1))
                        for h in range(NH):
                            if l < LEVELS - 1:
                                mm(banks4(3 * u + 1)[:, h], dR[:, u, h] if l else ident[:], dP[:, u, h], start=True, stop=True)
                        for h in range(NH):
                            ins = mm(banks4(3 * u + 2)[:, h], dP[:, u, h], dR[:, u, h] if l else ident[:], start=True, stop=True)
                        ins.then_inc(s_xy, 1)
                pe.wait_ge(s_a1, i * 2 + 2)
                for u in range(2):
                    pe.wait_ge(s_du, i * 12 + (2 * LEVELS - 1 + u))
                    for h in range(NH):
                        ins = mm(banks4(3 * u)[:, h], kbg[:, u, h], dR[:, u, h], start=True, stop=True)
                    ins.then_inc(s_w, 1)
                for c in range(4):
                    u, cols = c // 2, slice(CHUNK * (c % 2), CHUNK * (c % 2 + 1))
                    if c % 2 == 0:
                        pe.wait_ge(s_wn, i * 2 + (u + 1))
                    pe.wait_ge(s_su, i * 4 + (c + 1))
                    for h in range(NH):
                        mm(banks4(6)[:, h], dR[:, u, h], vb[:, u, h], start=True, stop=False)
                        ins = mm(banks4(6)[:, h], wTn[:, u, h], S[:, h], start=False, stop=True)
                    ins.then_inc(s_v, 1)
                    pe.wait_ge(s_vn, i * 4 + (c + 1))
                    pe.wait_ge(s_oev, i * 4 + (c + 1))
                    for h in range(NH):
                        o = ps[7][:, h * CHUNK:(h + 1) * CHUNK]
                        mm(o, S[:, h], qdec[:, u, h, cols], start=True, stop=False)
                        ins = mm(o, vn[:, c % 2, h], AT[:, u, h, cols], start=False, stop=True)
                    ins.then_inc(s_o, 1)
                    for h in range(NH):
                        ins = mm(banks4(c % 2)[:, h], kdec[:, u, h], vn[:, c % 2, h], start=True, stop=True)
                    ins.then_inc(s_sm, 1)
            for n in range(2 * NH):
                h, cols = n // 2, slice((n % 2) * HALF, (n % 2 + 1) * HALF)
                pe.wait_ge(s_oq, h + 1)
                if n == 0:
                    pe.wait_ge(s_su, 2 * NT + 1)
                if n >= 4:
                    pe.wait_ge(s_oa, n - 3)
                mm(ps[n % 4], ones[:], b_c[:, NH + h, cols], start=True, stop=True).then_inc(s_om, 1)
            phase_done(pe, "pe")
            def gate_branch(m, u, first):
                pe.wait_ge(s_gl, m + 1)
                for h in range(2):
                    cols = slice(h * HALF, (h + 1) * HALF)
                    if not first:
                        pe.wait_ge(s_mg, m * 2 + (h - 3))
                    for k in range(KD):
                        ins = mm3(ps[4 * u + 2 * h], g_h[:, u, k], g_l[:, u, k], hT_h[:, k, cols], hT_l[:, k, cols], k == 0, k == KD - 1)
                    ins.then_inc(s_pm, 1)
                    for k in range(NH):
                        ins = mm3(ps[4 * u + 2 * h + 1], br_h[:, u, k], br_l[:, u, k], y_h[:, k, cols], y_l[:, k, cols], k == 0, k == NH - 1)
                    ins.then_inc(s_pm, 1)

            for br in range(3):
                pe.wait_ge(s_yl2, NH * (br + 1))
                if br == 0:
                    for u in range(2):
                        gate_branch(u, u, True)
                with pe.Fori(1 if br == 0 else 0, NB // 2) as i:
                    for u in range(2):
                        gate_branch(i * 2 + (br * NB + u), u, False)
            phase_done(pe, "pe")
            pe.wait_ge(s_ml, KD)
            for c in range(4):
                pe.wait_ge(s_wol, c + 1)
                for g in range(4):
                    if c:
                        pe.wait_ge(s_x2, 4 * (c - 1) + g + 1)
                    for a in range(2):
                        t = slice((2 * g + a) * P, (2 * g + a + 1) * P)
                        for k in range(KD):
                            ins = mm3(ps[g][:, a * CW:(a + 1) * CW], m_h[:, k, t], m_l[:, k, t], wo_h[:, c % 2, k], wo_l[:, c % 2, k],
                                      k == 0, k == KD - 1)
                    ins.then_inc(s_po, 1)
            n = 0
            for t in range(NT):
                pe.wait_ge(s_xn2, t + 1)
                for q in range(2):
                    if n >= 4:
                        pe.wait_ge(s_h2, n - 3)
                    for j in range(4):
                        k = 4 * q + j
                        ins = nc.tensor.transpose(ps[n % 4][:, j * P:(j + 1) * P], xn2[:, t, k * P:(k + 1) * P], ident[:])
                    ins.then_inc(s_t2, 1)
                    n += 1
            pe.wait_ge(s_h2, 2 * NT)
            pe.wait_ge(s_rc, 16 * 5)
            for t in range(NT):
                for k in range(KD):
                    ins = mm(ps[4][:, t * 36:(t + 1) * 36], h2T[:, k, t * P:(t + 1) * P], wr[:, k], start=k == 0, stop=k == KD - 1)
            ins.then_inc(s_rm, 1)
            pe.wait_ge(s_rd1, ONE_HOTS)
            for t in range(NT + 1):
                o = ps[5][:, t * 32:(t + 1) * 32]
                for a in range(t):
                    ins = mm(o, ones[:], Osum[:, a], start=a == 0, stop=t == NT and a == NT - 1)
                if t < NT:
                    mm(o, strict[:], Osum[:, t], start=t == 0, stop=True)
            ins.then_inc(s_rk, 1)
            phase_done(pe, "pe")
            nb = pe.value_load(bexp[0:1, NBLK:NBLK + 1], min_val=2, max_val=NBLK)

            def up(b):
                pe.wait_ge(s_xl, b * 2 + 2)
                for c in range(4):
                    pe.wait_ge(s_el13, b * 4 + (c + 1))
                    if c % 2 == 0 and not (isinstance(b, int) and b == 0):
                        pe.wait_ge((s_si, s_hd)[c // 2], b)
                    for kk in range(4):
                        k, cols = 4 * (c % 2) + kk, slice(kk * FF, (kk + 1) * FF)
                        ins = mm3(ps[2 + c // 2], xT_h[:, k], xT_l[:, k], e_h[:, c, cols], e_l[:, c, cols], k == 0, k == KD - 1)
                    ins.then_inc(s_e13, 1)

            def rows_transposed(b, peeled):
                pe.wait_ge(s_xr, b + 1)
                for r in range(2):
                    if not peeled:
                        pe.wait_ge(s_xl, b * 2 + (r - 1))
                    for j in range(4):
                        k = 4 * r + j
                        ins = nc.tensor.transpose(ps[r][:, j * P:(j + 1) * P], xr[:, k * P:(k + 1) * P], ident[:])
                    ins.then_inc(s_tx, 1)

            def down(b):
                pe.wait_ge(s_hl2, b + 1)
                if not (isinstance(b, int) and b == 0):
                    pe.wait_ge(s_ye, b * 2)
                for c in range(4, 6):
                    pe.wait_ge(s_el2, b * 2 + (c - 3))
                    for kk in range(2):
                        k = 2 * (c - 4) + kk
                        for r in range(2):
                            cols = slice(kk * D + r * HALF, kk * D + (r + 1) * HALF)
                            ins = mm3(ps[4 + r], hT2_h[:, k], hT2_l[:, k], e_h[:, c, cols], e_l[:, c, cols], k == 0, k == 3)
                    ins.then_inc(s_e2, 1)

            def hidden_transposed(b):
                pe.wait_ge(s_hd, b + 1)
                if not (isinstance(b, int) and b == 0):
                    pe.wait_ge(s_hl2, b)
                for k in range(4):
                    ins = nc.tensor.transpose(banks4(6)[:, k], hid[:, k * P:(k + 1) * P], ident[:])
                ins.then_inc(s_th, 1)

            rows_transposed(0, True)
            up(0)
            rows_transposed(1, False)
            hidden_transposed(0)
            up(1)
            rows_transposed(2, False)
            down(0)
            hidden_transposed(1)
            with pe.Fori(2, NBLK - 1) as b:
                with pe.If(b < nb):
                    up(b)
                    with pe.If(b + 1 < nb):
                        rows_transposed(b + 1, False)
                    down(b - 1)
                    hidden_transposed(b)
                    with pe.If(b + 1 >= nb):
                        down(b)
            phase_done(pe, "pe")


def chunk_masks():
    j, i = np.arange(P)[:, None], np.arange(P)[None, :]
    same = j // CHUNK == i // CHUNK
    one = np.ones((P, P), bool)
    masks = [same & (j <= i), same, (j < CHUNK) & one, (j >= CHUNK) & one]
    for l in range(LEVELS):
        b = 1 << l
        masks.append((j // (2 * b) == i // (2 * b)) & (i // b % 2 == 1) & (j // b % 2 == 0))
    return np.ascontiguousarray(np.stack(masks, axis=1).astype(np.float32))


def layout_w_in(w):
    cols = [(512, 1024), (6152, 6664), (0, 512), (1024, 3072), (3080, 6152), (6664, 9736)]
    w2 = np.concatenate([w[:, a:b] for a, b in cols], axis=1)
    return np.ascontiguousarray(w2.reshape(KD, P, -1, CW).transpose(2, 1, 0, 3))


def router_constants():
    c = np.zeros((P, 96 + P), np.float32)
    c[:, 0:32] = np.arange(32)
    c[:, 32:80] = P * np.arange(48)
    c[:, 96:] = np.arange(P)[:, None] < np.arange(P)[None, :]
    return c


def kernel(**inputs):
    import concourse.bacc as bacc
    from concourse.bass_utils import run_bass_kernel_spmd

    a = {n: np.asarray(v) for n, v in inputs.items()}
    lay = np.ascontiguousarray
    w = a["w_in"][0]
    column = lambda v: lay(v.reshape(-1, P).T)
    tiles = lambda m, k: lay(m.reshape(KD, P, -1, k).transpose(2, 1, 0, 3))
    rows = dict(
        x=a["x"][0],
        w_in_t=layout_w_in(w),
        w_ba=lay(w[:, 3072:3080].reshape(KD, P, 8).transpose(1, 0, 2)),
        g_mix=column(a["norm_mix_g"][0]),
        a_ws_t=lay(a["a_w_s"][0].transpose(2, 0, 1)),
        a_bs=lay(a["a_b_s"][0].reshape(1, NC)),
        a_gb=lay(np.broadcast_to(np.stack([a["a_ln_g"][0], a["a_ln_b"][0]]), (P, 2, NC))),
        sel=bucket_selector(),
        relb=a["rel_bias"],
        conv_w=lay(a["b_conv_w"][0].reshape(4, 3 * NH, P).transpose(2, 1, 0)),
        b_hv=lay(np.broadcast_to(np.stack([a["b_a_log"][0], a["b_dt_bias"][0]]), (P, 2, NH))),
        b_ng=lay(a["b_norm_g"][0].reshape(P, 1)),
        b_masks=chunk_masks(),
        w_br=lay(a["w_branch"][0].reshape(3, NH, P, D // P, P).transpose(0, 3, 2, 1, 4)),
        w_o=tiles(a["w_out"][0], CW),
        g_ffn=column(a["norm_ffn_g"][0]),
        w_r=lay(np.concatenate([a["w_group"][0], a["w_expert"][0]], axis=1).reshape(KD, P, 36).transpose(1, 0, 2)),
        iotas=router_constants(),
        tok_ids=lay(np.arange(2 * T, dtype=np.int32).reshape(2, NT, P).transpose(2, 0, 1)),
        w1=a["w1"][0],
        w3=a["w3"][0],
        w2=a["w2"][0],
        g_fin=lay(np.broadcast_to(a["final_norm_g"], (P, D))),
    )
    nc = bacc.Bacc("TRN2", target_bir_lowering=False, num_devices=1)
    args = {n: nc.dram_tensor(f"in_{n}", v.shape, mybir.dt.from_np(v.dtype), kind="ExternalInput").ap() for n, v in rows.items()}
    out = nc.dram_tensor("out", (T, D), F32, kind="ExternalOutput").ap()
    build(nc, out=out, **args)
    r = run_bass_kernel_spmd(nc, [{f"in_{n}": v for n, v in rows.items()}], core_ids=[0])
    return r.results[0]["out"].reshape(1, T, D)
```
